# Optimizing a Trainium2 kernel written in Bass

```python
import math
import jax, jax.numpy as jnp
from jax import lax
import numpy as np

D_MODEL = 1024
BATCH = 1
SEQ = 512
DEPTH = 2

N_MIXERS = 4
NORM_EPS = 1e-6
NEG_INF = -1e30
D_FF = 2816

RET_HEADS = 4
RET_DK = D_MODEL // RET_HEADS
RET_DV = 2 * RET_DK
RET_CHUNK = 128
ROPE_BASE = 10000.0

NSA_HEADS = 16
NSA_GROUPS = 4
NSA_HPG = NSA_HEADS // NSA_GROUPS
NSA_DH = D_MODEL // NSA_HEADS
NSA_CMP_LEN = 32
NSA_CMP_STRIDE = 16
NSA_CMP_HID = 4 * NSA_DH
NSA_SEL_LEN = 64
NSA_N_SEL = 16
NSA_WINDOW = 512
NSA_Q_BLOCK = 32
NSA_FORCE_BONUS = 1e4

SSD_D_INNER = 2 * D_MODEL
SSD_HEADDIM = 64
SSD_HEADS = SSD_D_INNER // SSD_HEADDIM
SSD_GROUPS = 4
SSD_HPG = SSD_HEADS // SSD_GROUPS
SSD_STATE = 128
SSD_CONV = 4
SSD_CONV_DIM = SSD_D_INNER + 2 * SSD_GROUPS * SSD_STATE
SSD_CHUNK = 256

DIL_PATTERN = ((128, 1), (512, 4), (2048, 16))
DIL_HEADS = 8
DIL_DH = D_MODEL // DIL_HEADS
DIL_Q_BLOCK = 128

kernel_name = "hybrid_interleaved_retnet_nsa_ssd_dilated"

def _rmsnorm(x, g):
    xf = x.astype(jnp.float32)
    y = xf * lax.rsqrt(jnp.mean(xf * xf, axis=-1, keepdims=True) + NORM_EPS)
    return (y * g.astype(jnp.float32)).astype(x.dtype)

def _swiglu(u, w_in, w_out):
    a, b = jnp.split(u @ w_in, 2, axis=-1)
    return (jax.nn.silu(a) * b) @ w_out

def _masked_softmax(s, mask):
    s = jnp.where(mask, s.astype(jnp.float32), NEG_INF)
    m = jnp.max(s, axis=-1, keepdims=True)
    e = jnp.where(mask, jnp.exp(s - m), 0.0)
    den = jnp.maximum(jnp.sum(e, axis=-1, keepdims=True), 1e-30)
    return e / den, (m + jnp.log(den))[..., 0]

def _rotary(t, pos):
    half = t.shape[-1] // 2
    inv = ROPE_BASE ** (-jnp.arange(half, dtype=jnp.float32) / half)
    ang = pos.astype(jnp.float32)[:, None] * inv[None, :]
    cos = jnp.cos(ang)[None, :, None, :]
    sin = jnp.sin(ang)[None, :, None, :]
    tf = t.astype(jnp.float32)
    t1, t2 = tf[..., :half], tf[..., half:]
    return jnp.concatenate([t1 * cos - t2 * sin, t1 * sin + t2 * cos], axis=-1).astype(t.dtype)

def _retention(u, w_in, gn_gain, w_out):
    b, s, _ = u.shape
    hk, hv = RET_HEADS * RET_DK, RET_HEADS * RET_DV
    q, k, v, g = jnp.split(u @ w_in, [hk, 2 * hk, 2 * hk + hv], axis=-1)
    pos = jnp.arange(s)
    q = _rotary(q.reshape(b, s, RET_HEADS, RET_DK), pos)
    k = _rotary(k.reshape(b, s, RET_HEADS, RET_DK), pos) * (RET_DK ** -0.5)
    v = v.reshape(b, s, RET_HEADS, RET_DV)
    n_ch = s // RET_CHUNK

    def to_chunks(t):
        return t.astype(jnp.float32).reshape(b, n_ch, RET_CHUNK, RET_HEADS, -1).transpose(1, 0, 3, 2, 4)

    log_gamma = jnp.log1p(-jnp.exp2(-5.0 - jnp.arange(RET_HEADS, dtype=jnp.float32)))
    idx = jnp.arange(RET_CHUNK, dtype=jnp.float32)
    rel = idx[:, None] - idx[None, :]
    causal = rel >= 0
    inner_decay = jnp.where(causal, jnp.exp(jnp.where(causal, rel, 0.0) * log_gamma[:, None, None]), 0.0)
    q_decay = jnp.exp((idx + 1.0) * log_gamma[:, None])[None, :, :, None]
    k_decay = jnp.exp((RET_CHUNK - 1.0 - idx) * log_gamma[:, None])[None, :, :, None]
    chunk_decay = jnp.exp(RET_CHUNK * log_gamma)[None, :, None, None]

    def step(state, qkv):
        qc, kc, vc = qkv
        sc = jnp.einsum('bhid,bhjd->bhij', qc, kc) * inner_decay
        o = jnp.einsum('bhij,bhje->bhie', sc, vc) + jnp.einsum('bhid,bhde->bhie', qc, state) * q_decay
        state = state * chunk_decay + jnp.einsum('bhjd,bhje->bhde', kc * k_decay, vc)
        return state, o

    state0 = jnp.zeros((b, RET_HEADS, RET_DK, RET_DV), jnp.float32)
    _, o = lax.scan(step, state0, (to_chunks(q), to_chunks(k), to_chunks(v)))
    o = o.transpose(1, 0, 3, 2, 4).reshape(b, s, RET_HEADS, RET_DV)
    o = _rmsnorm(o, gn_gain.reshape(RET_HEADS, RET_DV)).astype(u.dtype).reshape(b, s, hv)
    return (jax.nn.silu(g) * o) @ w_out

def _nsa(u, w_in, cmp_pos, cmp_w1, cmp_w2, w_out):
    b, s, _ = u.shape
    G, HPG, DH, QB = NSA_GROUPS, NSA_HPG, NSA_DH, NSA_Q_BLOCK
    hq, hkv = NSA_HEADS * DH, G * DH
    q, kv, gates = jnp.split(u @ w_in, [hq, hq + 6 * hkv], axis=-1)
    q = q.reshape(b, s, G, HPG, DH).transpose(0, 2, 3, 1, 4)
    kv = kv.reshape(b, s, 3, 2, G, DH).transpose(2, 3, 0, 4, 1, 5)
    gates = jax.nn.sigmoid(gates.reshape(b, s, 3, G, HPG).transpose(2, 0, 3, 4, 1))
    scale = DH ** -0.5

    n_cmp = (s - NSA_CMP_LEN) // NSA_CMP_STRIDE + 1
    blk = jnp.arange(n_cmp)[:, None] * NSA_CMP_STRIDE + jnp.arange(NSA_CMP_LEN)[None, :]

    def compress(t, c):
        tb = t[:, :, blk, :] + cmp_pos[c]
        hid = jax.nn.silu(tb.reshape(b, G, n_cmp, NSA_CMP_LEN * DH) @ cmp_w1[c])
        return hid @ cmp_w2[c]

    k_cmp, v_cmp = compress(kv[0, 0], 0), compress(kv[0, 1], 1)
    cmp_end = jnp.arange(n_cmp) * NSA_CMP_STRIDE + NSA_CMP_LEN - 1

    nb = s // NSA_SEL_LEN
    n_sel = min(NSA_N_SEL, nb)
    k_sel = kv[1, 0].reshape(b, G, nb, NSA_SEL_LEN, DH)
    v_sel = kv[1, 1].reshape(b, G, nb, NSA_SEL_LEN, DH)
    ratio = NSA_SEL_LEN // NSA_CMP_STRIDE
    span = NSA_CMP_LEN // NSA_CMP_STRIDE
    pad_r = ratio * nb + ratio + 1 - n_cmp
    gather = jax.vmap(jax.vmap(lambda tb, ib: tb[ib]))

    pad_w = ((0, 0), (0, 0), (NSA_WINDOW, 0), (0, 0))
    k_win, v_win = jnp.pad(kv[2, 0], pad_w), jnp.pad(kv[2, 1], pad_w)

    def block(c):
        t0 = c * QB
        t = t0 + jnp.arange(QB)
        qc = lax.dynamic_slice_in_dim(q, t0, QB, axis=3)
        gc = lax.dynamic_slice_in_dim(gates, t0, QB, axis=4)
        s_c = jnp.einsum('bghqd,bgnd->bghqn', qc, k_cmp) * scale
        p_c, _ = _masked_softmax(s_c, cmp_end[None, :] <= t[:, None])
        o_c = jnp.einsum('bghqn,bgnd->bghqd', p_c.astype(v_cmp.dtype), v_cmp)
        imp = jnp.pad(p_c.sum(axis=2), ((0, 0), (0, 0), (0, 0), (span - 1, pad_r)))
        imp_sel = 0.0
        for m in range(ratio):
            for n in range(span):
                imp_sel = imp_sel + imp[..., m + n: m + n + ratio * nb: ratio]
        cur = (t // NSA_SEL_LEN)[:, None]
        jb = jnp.arange(nb)[None, :]
        forced = (jb == 0) | (jb == cur) | (jb == cur - 1)
        score = jnp.where(jb <= cur, imp_sel + jnp.where(forced, NSA_FORCE_BONUS, 0.0), NEG_INF)
        top_val, top_idx = lax.top_k(score, n_sel)
        valid = top_val > 0.5 * NEG_INF
        k_g = gather(k_sel, top_idx).reshape(b, G, QB, n_sel * NSA_SEL_LEN, DH)
        v_g = gather(v_sel, top_idx).reshape(b, G, QB, n_sel * NSA_SEL_LEN, DH)
        key_pos = top_idx[..., None] * NSA_SEL_LEN + jnp.arange(NSA_SEL_LEN)
        m_sel = (valid[..., None] & (key_pos <= t[:, None, None])).reshape(b, G, 1, QB, n_sel * NSA_SEL_LEN)
        s_s = jnp.einsum('bghqd,bgqkd->bghqk', qc, k_g) * scale
        p_s, _ = _masked_softmax(s_s, m_sel)
        o_s = jnp.einsum('bghqk,bgqkd->bghqd', p_s.astype(v_g.dtype), v_g)
        kw = lax.dynamic_slice_in_dim(k_win, t0, NSA_WINDOW + QB, axis=2)
        vw = lax.dynamic_slice_in_dim(v_win, t0, NSA_WINDOW + QB, axis=2)
        kpos = (t0 - NSA_WINDOW + jnp.arange(NSA_WINDOW + QB))[None, :]
        m_w = (kpos <= t[:, None]) & (kpos > t[:, None] - NSA_WINDOW) & (kpos >= 0)
        s_w = jnp.einsum('bghqd,bgkd->bghqk', qc, kw) * scale
        p_w, _ = _masked_softmax(s_w, m_w)
        o_w = jnp.einsum('bghqk,bgkd->bghqd', p_w.astype(vw.dtype), vw)
        return gc[0][..., None] * o_c + gc[1][..., None] * o_s + gc[2][..., None] * o_w

    out = lax.map(block, jnp.arange(s // QB))
    out = out.transpose(1, 0, 4, 2, 3, 5).reshape(b, s, hq)
    return out.astype(u.dtype) @ w_out

def _ssd(u, w_in, conv_w, conv_b, dt_bias, a_log, d_skip, norm_g, w_out):
    b, s, _ = u.shape
    G, R, P, N, L = SSD_GROUPS, SSD_HPG, SSD_HEADDIM, SSD_STATE, SSD_CHUNK
    f32 = jnp.float32
    z, xbc, dt = jnp.split(u @ w_in, [SSD_D_INNER, SSD_D_INNER + SSD_CONV_DIM], axis=-1)
    xp = jnp.pad(xbc, ((0, 0), (SSD_CONV - 1, 0), (0, 0)))
    conv = conv_b
    for k in range(SSD_CONV):
        conv = conv + xp[:, k:k + s] * conv_w[k]
    xbc = jax.nn.silu(conv)
    xs, bm, cm = jnp.split(xbc, [SSD_D_INNER, SSD_D_INNER + G * N], axis=-1)
    xs = xs.astype(f32).reshape(b, s, G, R, P)
    bm = bm.astype(f32).reshape(b, s, G, N)
    cm = cm.astype(f32).reshape(b, s, G, N)
    dt = jax.nn.softplus(dt.astype(f32) + dt_bias.astype(f32)).reshape(b, s, G, R)
    A = -jnp.exp(a_log.astype(f32)).reshape(G, R)
    n_ch = -(-s // L)
    pad = n_ch * L - s

    def to_chunks(t):
        t = jnp.pad(t, ((0, 0), (0, pad)) + ((0, 0),) * (t.ndim - 2))
        return t.reshape((b, n_ch, L) + t.shape[2:]).swapaxes(0, 1)

    causal = jnp.tril(jnp.ones((L, L), bool))[None, :, :, None, None]

    def step(state, inp):
        xc, dtc, bc, cc = inp
        acs = jnp.cumsum(dtc * A, axis=1)
        seg = jnp.where(causal, jnp.exp(jnp.where(causal, acs[:, :, None] - acs[:, None, :], 0.0)), 0.0)
        cb = jnp.einsum('bign,bjgn->bijg', cc, bc)
        w = cb[..., None] * seg * dtc[:, None]
        y = jnp.einsum('bijgr,bjgrp->bigrp', w, xc)
        y = y + jnp.einsum('bign,bgrpn->bigrp', cc, state) * jnp.exp(acs)[..., None]
        to_end = jnp.exp(acs[:, -1:] - acs) * dtc
        state = state * jnp.exp(acs[:, -1])[..., None, None] + jnp.einsum('bjgn,bjgr,bjgrp->bgrpn', bc, to_end, xc)
        return state, y

    state0 = jnp.zeros((b, G, R, P, N), f32)
    _, y = lax.scan(step, state0, (to_chunks(xs), to_chunks(dt), to_chunks(bm), to_chunks(cm)))
    y = y.swapaxes(0, 1).reshape(b, n_ch * L, G, R, P)[:, :s]
    y = y + d_skip.astype(f32).reshape(G, R)[..., None] * xs
    yz = y.reshape(b, s, G, R * P) * jax.nn.silu(z.astype(f32)).reshape(b, s, G, R * P)
    y = _rmsnorm(yz, norm_g.reshape(G, R * P)).reshape(b, s, SSD_D_INNER).astype(u.dtype)
    return y @ w_out

def _dilated_group(q, k, v, r, n_back):
    b, s, h, dh = q.shape
    QB = DIL_Q_BLOCK
    L = s // r
    nb = -(-L // QB)
    Lp = nb * QB

    def to_sub(t):
        t = t.reshape(b, L, r, h, dh).transpose(0, 2, 3, 1, 4)
        return jnp.pad(t, ((0, 0), (0, 0), (0, 0), (0, Lp - L), (0, 0)))

    def band(t):
        tp = jnp.pad(to_sub(t), ((0, 0), (0, 0), (0, 0), (QB, 0), (0, 0))).reshape(b, r, h, nb + 1, QB, dh)
        return jnp.concatenate([tp[:, :, :, :-1], tp[:, :, :, 1:]], axis=4)

    qs = to_sub(q).reshape(b, r, h, nb, QB, dh)
    kb, vb = band(k), band(v)
    qi = jnp.arange(QB)[:, None]
    kj = jnp.arange(2 * QB)[None, :]
    dist = qi + QB - kj
    key_sub = jnp.arange(nb)[:, None, None] * QB - QB + kj[None]
    mask = (dist >= 0) & (dist <= n_back) & (key_sub >= 0)
    sc = jnp.einsum('bchnqd,bchnkd->bchnqk', qs, kb) * (dh ** -0.5)
    p, lse = _masked_softmax(sc, mask)
    o = jnp.einsum('bchnqk,bchnkd->bchnqd', p.astype(vb.dtype), vb)
    o = o.reshape(b, r, h, Lp, dh)[:, :, :, :L].transpose(0, 3, 1, 2, 4).reshape(b, s, h, dh)
    lse = lse.reshape(b, r, h, Lp)[:, :, :, :L].transpose(0, 3, 1, 2).reshape(b, s, h)
    return o, lse

def _dilated(u, w_in, w_out):
    b, s, _ = u.shape
    proj = (u @ w_in).reshape(b, s, len(DIL_PATTERN), 3, DIL_HEADS, DIL_DH)
    outs, lses = [], []
    for g, (win, r) in enumerate(DIL_PATTERN):
        o, lse = _dilated_group(proj[:, :, g, 0], proj[:, :, g, 1], proj[:, :, g, 2], r, win // r)
        outs.append(o)
        lses.append(lse)
    wts = jax.nn.softmax(jnp.stack(lses), axis=0)
    o = jnp.einsum('gbsh,gbshd->bshd', wts.astype(u.dtype), jnp.stack(outs))
    return o.reshape(b, s, DIL_HEADS * DIL_DH) @ w_out

def setup_inputs(seed: int = 0) -> dict:
    key = jax.random.key(seed)
    ks = iter(jax.random.split(key, 32))
    f32 = jnp.float32

    def nrm(shape, scale):
        return jax.random.normal(next(ks), shape, f32) * scale

    def gain(shape):
        return 1.0 + 0.01 * jax.random.normal(next(ks), shape, f32)

    n_a, n_b, n_c, n_d = (len(range(m, DEPTH, N_MIXERS)) for m in range(N_MIXERS))
    dt0 = jnp.exp(jax.random.uniform(next(ks), (n_c, SSD_HEADS), f32, math.log(1e-3), math.log(1e-1)))
    return {
        "x": nrm((BATCH, SEQ, D_MODEL), 1.0),
        "norm_ffn1": gain((DEPTH, D_MODEL)),
        "ffn1_w_in": nrm((DEPTH, D_MODEL, 2 * D_FF), D_MODEL ** -0.5),
        "ffn1_w_out": nrm((DEPTH, D_FF, D_MODEL), D_FF ** -0.5),
        "norm_mix": gain((DEPTH, D_MODEL)),
        "norm_ffn2": gain((DEPTH, D_MODEL)),
        "ffn2_w_in": nrm((DEPTH, D_MODEL, 2 * D_FF), D_MODEL ** -0.5),
        "ffn2_w_out": nrm((DEPTH, D_FF, D_MODEL), D_FF ** -0.5),
        "norm_final": gain((D_MODEL,)),
        "ret_w_in": nrm((n_a, D_MODEL, 2 * RET_HEADS * RET_DK + 2 * RET_HEADS * RET_DV), D_MODEL ** -0.5),
        "ret_gn_gain": gain((n_a, RET_HEADS * RET_DV)),
        "ret_w_out": nrm((n_a, RET_HEADS * RET_DV, D_MODEL), (RET_HEADS * RET_DV) ** -0.5),
        "nsa_w_in": nrm((n_b, D_MODEL, NSA_HEADS * NSA_DH + 6 * NSA_GROUPS * NSA_DH + 3 * NSA_HEADS), D_MODEL ** -0.5),
        "nsa_cmp_pos": nrm((n_b, 2, NSA_CMP_LEN, NSA_DH), 0.02),
        "nsa_cmp_w1": nrm((n_b, 2, NSA_CMP_LEN * NSA_DH, NSA_CMP_HID), (NSA_CMP_LEN * NSA_DH) ** -0.5),
        "nsa_cmp_w2": nrm((n_b, 2, NSA_CMP_HID, NSA_DH), NSA_CMP_HID ** -0.5),
        "nsa_w_out": nrm((n_b, NSA_HEADS * NSA_DH, D_MODEL), (NSA_HEADS * NSA_DH) ** -0.5),
        "ssd_w_in": nrm((n_c, D_MODEL, SSD_D_INNER + SSD_CONV_DIM + SSD_HEADS), D_MODEL ** -0.5),
        "ssd_conv_w": nrm((n_c, SSD_CONV, SSD_CONV_DIM), SSD_CONV ** -0.5),
        "ssd_conv_b": nrm((n_c, SSD_CONV_DIM), 0.01),
        "ssd_dt_bias": dt0 + jnp.log(-jnp.expm1(-dt0)),
        "ssd_a_log": jnp.log(jax.random.uniform(next(ks), (n_c, SSD_HEADS), f32, 1.0, 16.0)),
        "ssd_d": gain((n_c, SSD_HEADS)),
        "ssd_norm": gain((n_c, SSD_D_INNER)),
        "ssd_w_out": nrm((n_c, SSD_D_INNER, D_MODEL), SSD_D_INNER ** -0.5),
        "dil_w_in": nrm((n_d, D_MODEL, len(DIL_PATTERN) * 3 * DIL_HEADS * DIL_DH), D_MODEL ** -0.5),
        "dil_w_out": nrm((n_d, DIL_HEADS * DIL_DH, D_MODEL), (DIL_HEADS * DIL_DH) ** -0.5),
    }

def reference(x, norm_ffn1, ffn1_w_in, ffn1_w_out, norm_mix, norm_ffn2, ffn2_w_in, ffn2_w_out, norm_final,
              ret_w_in, ret_gn_gain, ret_w_out,
              nsa_w_in, nsa_cmp_pos, nsa_cmp_w1, nsa_cmp_w2, nsa_w_out,
              ssd_w_in, ssd_conv_w, ssd_conv_b, ssd_dt_bias, ssd_a_log, ssd_d, ssd_norm, ssd_w_out,
              dil_w_in, dil_w_out):
    h = x
    for i in range(DEPTH):
        h = h + 0.5 * _swiglu(_rmsnorm(h, norm_ffn1[i]), ffn1_w_in[i], ffn1_w_out[i])
        u = _rmsnorm(h, norm_mix[i])
        m, j = i % N_MIXERS, i // N_MIXERS
        if m == 0:
            y = _retention(u, ret_w_in[j], ret_gn_gain[j], ret_w_out[j])
        elif m == 1:
            y = _nsa(u, nsa_w_in[j], nsa_cmp_pos[j], nsa_cmp_w1[j], nsa_cmp_w2[j], nsa_w_out[j])
        elif m == 2:
            y = _ssd(u, ssd_w_in[j], ssd_conv_w[j], ssd_conv_b[j], ssd_dt_bias[j], ssd_a_log[j],
                     ssd_d[j], ssd_norm[j], ssd_w_out[j])
        else:
            y = _dilated(u, dil_w_in[j], dil_w_out[j])
        h = h + y
        h = h + 0.5 * _swiglu(_rmsnorm(h, norm_ffn2[i]), ffn2_w_in[i], ffn2_w_out[i])
    return _rmsnorm(h, norm_final)


_drawn_inputs = setup_inputs


def setup_inputs(seed=0):
    import zlib

    import numpy as np

    out = dict(_drawn_inputs(seed))
    spreads = {}
    factors = {'norm_ffn1': 7.959,
     'norm_mix': 4.65,
     'norm_ffn2': 101.533,
     'norm_final': 185.46,
     'ret_gn_gain': 135.908,
     'nsa_cmp_pos': 200.0,
     'nsa_w_in': 4.868,
     'nsa_cmp_w1': 8.0,
     'nsa_cmp_w2': 8.0,
     'nsa_w_out': 4.745}
    for name, (base, spread) in spreads.items():
        noise = np.random.default_rng([zlib.crc32(name.encode()), seed]).standard_normal(out[name].shape)
        drawn = base * np.exp(spread * noise) if base else spread * noise
        out[name] = __import__('jax').numpy.asarray(drawn.astype(out[name].dtype))
    for name, factor in factors.items():
        out[name] = (out[name] * factor).astype(out[name].dtype)
    return out
```

```python
from contextlib import ExitStack

import numpy as np

import concourse.bass as bass
import concourse.mybir as mybir

F32 = mybir.dt.float32
F32R = mybir.dt.float32r
BF16 = mybir.dt.bfloat16
ACT = mybir.ActivationFunctionType
ALU = mybir.AluOpType
AX_X = mybir.AxisListType.X
ds = bass.ds

P = 128
SEQ = 512
D_MODEL = 1024
D_FF = 2816
NORM_EPS = 1e-6
TOK_TILES = SEQ // P
D_TILES = D_MODEL // P
UNIT = 2048
PAIR = 2 * P
FF_PAIRS = D_FF // PAIR

RET_HEADS = 4
RET_DK = D_MODEL // RET_HEADS
RET_DV = 2 * RET_DK
RET_E_TILES = RET_DV // P
RET_K0 = RET_HEADS * RET_DK
RET_V0 = 2 * RET_K0
RET_G0 = RET_V0 + RET_HEADS * RET_DV

NSA_HEADS = 16
NSA_GROUPS = 4
NSA_HPG = NSA_HEADS // NSA_GROUPS
NSA_DH = D_MODEL // NSA_HEADS
NSA_KV0 = NSA_HEADS * NSA_DH
NSA_HKV = NSA_GROUPS * NSA_DH
NSA_GATE0 = NSA_KV0 + 6 * NSA_HKV
N_GATES = 3 * NSA_HEADS
CMP_LEN = 32
CMP_STRIDE = 16
CMP_HID = 4 * NSA_DH
N_CMP = (SEQ - CMP_LEN) // CMP_STRIDE + 1
CMP_PAD = 32
CMP_K_TILES = CMP_LEN * NSA_DH // P
NSA_SCALE = NSA_DH ** -0.5
NEG_RAW = -1e30 / NSA_SCALE
SEL_LEN, N_SEL, WINDOW = 64, 16, 512
assert SEQ // SEL_LEN <= N_SEL and SEQ <= WINDOW

FFN_USES = (FF_PAIRS,) * 3
RET_USES = (3 * RET_HEADS, 3 * RET_HEADS, 2 * RET_HEADS)
NSA_USES = (1 + NSA_GROUPS,) * 3
PHASE_USES = [FFN_USES, RET_USES, FFN_USES, FFN_USES, NSA_USES, FFN_USES]
QUARTERS = 4
PHASE_OUT = [D_TILES * n for n in (FF_PAIRS, RET_HEADS, FF_PAIRS, FF_PAIRS, NSA_GROUPS, FF_PAIRS)]
N_PHASES = len(PHASE_USES)
FFN_NO = {0: 0, 2: 1, 3: 2, 5: 3}
RET_PHASE, NSA_PHASE = 1, 4
USES0 = [[sum(u[s] for u in PHASE_USES[:ph]) for s in range(3)] for ph in range(N_PHASES)]
OUT0 = [sum(PHASE_OUT[:ph]) for ph in range(N_PHASES + 1)]
OUT_READY0 = [n // D_TILES * (D_TILES - 1) for n in OUT0]

ROW_NORM = [0, 16, 32, 8, 24, 40, 48]
ROW_GN = 56
ROW_POS = 72
N_ROWS = ROW_POS + 2 * CMP_K_TILES


ITEMS = [(pair, ib, par, br) for pair in range(2) for ib in range(TOK_TILES) for par in range(2) for br in range(2)]
N_ITEMS = len(ITEMS)
CS_STEPS = 10
GROUP_SETS = 9
N_CONST_LOADS = 13
MID_SQUARES = RET_HEADS * RET_E_TILES


def squares_before(m):
    return D_TILES * m + (MID_SQUARES if m > RET_PHASE else 0)


def norms_before(m):
    return m + (RET_HEADS if m > RET_PHASE else 0)


def sums_before(m):
    return (D_TILES - 1) * m + ((RET_E_TILES - 1) * RET_HEADS if m > RET_PHASE else 0)


def width(ib):
    return (ib + 1) * P


def build(nc, t):
    ctx = ExitStack()

    def sb(name, shape, dt=F32):
        return ctx.enter_context(nc.sbuf_tensor(name, shape, dt))

    def sem(name):
        return ctx.enter_context(nc.semaphore(name))

    with ctx:
        staged = [sb(f"staged{s}", [P, UNIT]) for s in range(3)]
        w_hi = [sb(f"w_hi{s}", [P, UNIT], F32R) for s in range(3)]
        w_lo = [sb(f"w_lo{s}", [P, UNIT], F32R) for s in range(3)]
        h = sb("h", [P, D_TILES, SEQ])
        u_hi = sb("u_hi", [P, D_TILES, SEQ], F32R)
        u_lo = sb("u_lo", [P, D_TILES, SEQ], F32R)
        sq = sb("sq", [P, 2, SEQ])
        sq_sum = sb("sq_sum", [P, SEQ])
        u_f32 = sb("u_f32", [P, 3, SEQ])
        std = sb("std", [P, TOK_TILES])
        rstd = sb("rstd", [P, TOK_TILES])
        eps = sb("eps", [P, 1])
        ones = sb("ones", [P, 1])
        ident = sb("ident", [P, P])
        ident_bf = sb("ident_bf", [P, P], BF16)
        causal_neg = sb("causal_neg", [P, P])
        causal_neg_bf = sb("causal_neg_bf", [P, P], BF16)
        cmp_mask = sb("cmp_mask", [P, TOK_TILES, CMP_PAD])
        cmp_neg = sb("cmp_neg", [P, TOK_TILES, CMP_PAD])
        rows = sb("rows", [N_ROWS, P])
        cols = sb("cols", [P, N_ROWS])
        mid_hi = sb("mid_hi", [P, 4, SEQ], F32R)
        mid_lo = sb("mid_lo", [P, 4, SEQ], F32R)
        work = sb("work", [P, 12800])

        taken = {}

        def area(phase, size, *shape):
            at = taken.get(phase, 0)
            taken[phase] = at + size
            assert at + size <= 12800, phase
            v = work[:, at:at + size]
            if len(shape) == 2:
                v = v.rearrange("p (a b) -> p a b", a=shape[0])
            elif len(shape) == 3:
                v = v.rearrange("p (a b c) -> p a b c", a=shape[0], b=shape[1])
            return v

        x_tok = area("start", TOK_TILES * D_MODEL, TOK_TILES, D_MODEL)
        silu_a = area("ffn", 2 * SEQ, 2, SEQ)
        hid = area("ffn", 2 * SEQ, 2, SEQ)
        r_q = area("ret", 2 * SEQ, 2, SEQ)
        r_k = area("ret", 2 * SEQ, 2, SEQ)
        r_v = area("ret", TOK_TILES * SEQ, TOK_TILES, SEQ)
        r_silu_g = area("ret", RET_E_TILES * SEQ, RET_E_TILES, SEQ)
        r_og = area("ret", RET_E_TILES * SEQ, RET_E_TILES, SEQ)
        cos_t = area("ret", SEQ)
        sin_t = area("ret", SEQ)
        decay = area("ret", RET_HEADS * SEQ)
        r_p = area("ret", sum(SEQ - jb * P for jb in range(TOK_TILES)))
        r_p_at = [sum(SEQ - j * P for j in range(jb)) for jb in range(TOK_TILES)]
        taken["end"] = TOK_TILES * D_MODEL
        y = area("end", D_TILES * SEQ, D_TILES, SEQ)
        c_x = area("cmp", CMP_K_TILES * NSA_GROUPS * N_CMP, CMP_K_TILES, NSA_GROUPS, N_CMP)
        taken["cmp"] = taken["ffn"]
        c_w1 = area("cmp", 2 * CMP_K_TILES * CMP_HID, 2, CMP_K_TILES, CMP_HID)
        c_t = area("cmp", NSA_GROUPS * SEQ, NSA_GROUPS, SEQ)
        n_q = area("nsa", 2 * SEQ, 2, SEQ)
        n_k = area("nsa", 4 * SEQ, 2, 2, SEQ)
        n_v = area("nsa", TOK_TILES * 2 * 3 * NSA_DH, TOK_TILES, 2, 3 * NSA_DH)
        n_p = area("nsa", 3 * SEQ, 3, SEQ)
        n_pt = area("nsa", 2 * SEQ, 2, SEQ)
        c_s = area("nsa", 16 * CMP_PAD, 16, CMP_PAD)
        c_p = area("nsa", 16 * CMP_PAD, 16, CMP_PAD)
        c_pt = area("nsa", 4 * P, 4, P)
        c_kg = area("nsa", 2 * CMP_PAD, 2, CMP_PAD)
        c_vg = area("nsa", TOK_TILES * 3 * NSA_DH, TOK_TILES, 3 * NSA_DH)
        gate_g = area("nsa", 3 * 16, 3, 16)
        c_max = area("nsa", 16)
        c_den = area("nsa", 16)
        c_rden = area("nsa", 16)
        c_fac = area("nsa", 16)
        s_max = area("nsa", 4)
        s_bias = area("nsa", 4)
        s_den = area("nsa", 4)
        s_rden = area("nsa", 4)
        c_w2 = sb("c_w2", [P, 2, 2, 2 * NSA_DH])
        c_hid = sb("c_hid", [P, 2, NSA_GROUPS * N_CMP])
        c_k = sb("c_k", [P, NSA_GROUPS, CMP_PAD])
        c_v = sb("c_v", [CMP_PAD, NSA_GROUPS, NSA_DH])
        gates = sb("gates", [P, TOK_TILES, N_GATES])

        bank = [ctx.enter_context(nc.psum_tensor(f"bank{b}", [P, SEQ], F32)) for b in range(8)]

        loaded = [sem(f"loaded{s}") for s in range(3)]
        split_hi = [sem(f"split_hi{s}") for s in range(3)]
        split_lo = [sem(f"split_lo{s}") for s in range(3)]
        unit_used = [sem(f"unit_used{s}") for s in range(3)]
        const_loaded = sem("const_loaded")
        x_loaded = sem("x_loaded")
        const_set = sem("const_set")
        const_derived = sem("const_derived")
        rows_turned = sem("rows_turned")
        cols_ready = sem("cols_ready")
        x_turned = sem("x_turned")
        y_ready = sem("y_ready")
        y_turned = sem("y_turned")
        y_copied = [sem(f"y_copied{i}") for i in range(2)]
        stored = sem("stored")
        out_ready = sem("out_ready")
        h_added = sem("h_added")
        squared = sem("squared")
        sq_summed = sem("sq_summed")
        sumsq_ready = sem("sumsq_ready")
        std_ready = sem("std_ready")
        rstd_ready = sem("rstd_ready")
        rstd_spread = sem("rstd_spread")
        u_scaled = sem("u_scaled")
        u_hi_ready = sem("u_hi_ready")
        u_ready = sem("u_ready")
        a_ready = sem("a_ready")
        b_ready = sem("b_ready")
        silu_ready = sem("silu_ready")
        hid_ready = sem("hid_ready")
        mid_hi_ready = sem("mid_hi_ready")
        mid_ready = sem("mid_ready")
        ret_loaded = sem("ret_loaded")
        qk_ready = sem("qk_ready")
        rot_products = sem("rot_products")
        rotated = sem("rotated")
        v_ready = sem("v_ready")
        v_copied = sem("v_copied")
        scores_ready = sem("scores_ready")
        decayed = sem("decayed")
        g_ready = sem("g_ready")
        silu_g_ready = sem("silu_g_ready")
        o_ready = sem("o_ready")
        gated = sem("gated")
        normed = sem("normed")
        z_hi_ready = sem("z_hi_ready")
        z_ready = sem("z_ready")
        cmp_loaded = sem("cmp_loaded")
        ct_ready = sem("ct_ready")
        ct_copied = sem("ct_copied")
        cx_ready = sem("cx_ready")
        chid_ready = sem("chid_ready")
        chid_silu = sem("chid_silu")
        ckv_ready = sem("ckv_ready")
        ckv_zeroed = sem("ckv_zeroed")
        ckv_copied = sem("ckv_copied")
        gates_set = sem("gates_set")
        gq_ready = sem("gq_ready")
        gq_copied = sem("gq_copied")
        gk_ready = sem("gk_ready")
        gk_copied = sem("gk_copied")
        gv_ready = sem("gv_ready")
        gv_copied = sem("gv_copied")
        group_set = sem("group_set")
        halves_zeroed = sem("halves_zeroed")
        cs_ready = sem("cs_ready")
        cs_steps = sem("cs_steps")
        cs_exp = sem("cs_exp")
        cpt_ready = sem("cpt_ready")
        cpt_copied = sem("cpt_copied")
        s_ready = sem("s_ready")
        s_maxed = sem("s_maxed")
        s_biased = sem("s_biased")
        s_exp = sem("s_exp")
        s_recip = sem("s_recip")
        p_ready = sem("p_ready")
        pt_ready = sem("pt_ready")
        pt_copied = [sem(f"pt_copied{i}") for i in range(2)]
        pv_done = sem("pv_done")
        no_ready = sem("no_ready")
        no_hi_ready = sem("no_hi_ready")
        no_split = sem("no_split")

        def in_view(s):
            return s.rearrange("p (k c) -> p k c", k=D_TILES)

        def v_view(s):
            return s.rearrange("p (k c) -> p k c", k=4)

        def out_view(s):
            return s.rearrange("p (k c) -> p k c", k=2)

        def tiled(w):
            return w.rearrange("(k p) c -> p k c", p=P)

        ffn_w_in = {0: tiled(t["ffn1_w_in"][0]), 2: tiled(t["ffn2_w_in"][0]),
                    3: tiled(t["ffn1_w_in"][1]), 5: tiled(t["ffn2_w_in"][1])}
        ffn_w_out = {0: tiled(t["ffn1_w_out"][0]), 2: tiled(t["ffn2_w_out"][0]),
                     3: tiled(t["ffn1_w_out"][1]), 5: tiled(t["ffn2_w_out"][1])}
        ret_w_in = tiled(t["ret_w_in"][0])
        ret_w_out = tiled(t["ret_w_out"][0])
        nsa_w_in = tiled(t["nsa_w_in"][0])
        nsa_w_out = tiled(t["nsa_w_out"][0])

        block = ctx.enter_context(nc.Block())

        @block.sync
        def _(sp):
            def load(slot, use, pieces):
                if not isinstance(use, int) or use > 0:
                    sp.wait_ge(split_lo[slot], use)
                for dst, src in pieces:
                    sp.dma_start(dst, src).then_inc(loaded[slot], 16)

            def load_ffn(ph, j, pieces=1):
                s, n = USES0[ph], D_TILES // pieces
                load(0, s[0] + j, [(in_view(staged[0][:]), ffn_w_in[ph][:, :, ds(j * PAIR, PAIR)])])
                load(1, s[1] + j, [(in_view(staged[1][:])[:, k:k + n, :],
                                    ffn_w_in[ph][:, k:k + n, ds(j * PAIR + D_FF, PAIR)])
                                   for k in range(0, D_TILES, n)])
                load(2, s[2] + j, [(out_view(staged[2][:]), ffn_w_out[ph][:, ds(j * 2, 2), :])])

            def load_ret(hd):
                s = USES0[RET_PHASE]
                load(0, s[0] + hd * 3, [(in_view(staged[0][:]), ret_w_in[:, :, ds(hd * RET_DK, PAIR)])])
                load(1, s[1] + hd * 3, [(in_view(staged[1][:]), ret_w_in[:, :, ds(hd * RET_DK + RET_K0, PAIR)])])
                load(2, s[2] + hd * 2, [(v_view(staged[2][:]), ret_w_in[:, 0:4, ds(hd * RET_DV + RET_V0, RET_DV)])])
                load(0, s[0] + hd * 3 + 1, [(v_view(staged[0][:]), ret_w_in[:, 4:8, ds(hd * RET_DV + RET_V0, RET_DV)])])
                load(1, s[1] + hd * 3 + 1, [(in_view(staged[1][:]), ret_w_in[:, :, ds(hd * RET_DV + RET_G0, PAIR)])])
                load(2, s[2] + hd * 2 + 1,
                     [(in_view(staged[2][:]), ret_w_in[:, :, ds(hd * RET_DV + (RET_G0 + PAIR), PAIR)])])
                load(0, s[0] + hd * 3 + 2, [(out_view(staged[0][:]), ret_w_out[:, ds(hd * 4, 2), :])])
                load(1, s[1] + hd * 3 + 2, [(out_view(staged[1][:]), ret_w_out[:, ds(hd * 4 + 2, 2), :])])

            def load_nsa(g, s):
                load(0, s[0] + g, [(in_view(staged[0][:]), nsa_w_in[:, :, ds(g * PAIR, PAIR)])])
                load(1, s[1] + g, [(in_view(staged[1][:])[:, :, i * NSA_DH:(i + 1) * NSA_DH],
                                    nsa_w_in[:, :, ds(g * NSA_DH + (NSA_KV0 + c * NSA_HKV), NSA_DH)])
                                   for i, c in enumerate((2, 4, 3, 5))])
                load(2, s[2] + g, [(out_view(staged[2][:]), nsa_w_out[:, ds(g * 2, 2), :])])

            sp.dma_start(ident[:], t["c_ident"]).then_inc(const_loaded, 16)
            src = t["x"][0].rearrange("(a p) d -> p a d", p=P)
            for a in range(TOK_TILES):
                sp.dma_start(x_tok[:, a, :], src[:, a, :]).then_inc(x_loaded, 16)
            load(0, 0, [(in_view(staged[0][:]), ffn_w_in[0][:, :, 0:PAIR])])
            at = 0
            for name in ("norm_ffn1", "norm_mix", "norm_ffn2"):
                sp.dma_start(rows[at:at + 16, :], t[name].rearrange("l (d p) -> (l d) p", p=P)).then_inc(const_loaded, 16)
                at += 16
            sp.dma_start(rows[at:at + 8, :], t["norm_final"].rearrange("(d p) -> d p", p=P)).then_inc(const_loaded, 16)
            sp.dma_start(rows[ROW_GN:ROW_GN + 16, :], t["ret_gn_gain"][0].rearrange("(d p) -> d p", p=P))\
              .then_inc(const_loaded, 16)
            sp.dma_start(rows[ROW_POS:N_ROWS, :],
                         t["nsa_cmp_pos"][0].rearrange("c (k l) d -> (c k) (l d)", l=2)).then_inc(const_loaded, 16)
            sp.dma_start(causal_neg[:], t["c_causal"]).then_inc(const_loaded, 16)
            sp.dma_start(cmp_mask[:], t["c_cmp_mask"]).then_inc(const_loaded, 16)
            for c in range(2):
                for i in range(2):
                    sp.dma_start(c_w2[:, c, :, i * NSA_DH:(i + 1) * NSA_DH],
                                 tiled(t["nsa_cmp_w2"][0, c])).then_inc(const_loaded, 16)

            def rest_of_first():
                load(1, 0, [(in_view(staged[1][:]), ffn_w_in[0][:, :, D_FF:D_FF + PAIR])])
                load(2, 0, [(out_view(staged[2][:]), ffn_w_out[0][:, 0:2, :])])

            rest_of_first()
            with sp.Fori(1, FF_PAIRS) as j:
                load_ffn(0, j)
            sp.dma_start(cos_t, t["c_cos"]).then_inc(ret_loaded, 16)
            sp.dma_start(sin_t, t["c_sin"]).then_inc(ret_loaded, 16)
            sp.dma_start(decay, t["c_decay"]).then_inc(ret_loaded, 16)
            with sp.Fori(0, RET_HEADS) as hd:
                load_ret(hd)
            with sp.Fori(0, FF_PAIRS) as j:
                load_ffn(2, j)
            sp.wait_ge(h_added, D_TILES + OUT0[RET_PHASE + 1])
            for c in range(2):
                sp.dma_start(c_w1[:, c, :, :], tiled(t["nsa_cmp_w1"][0, c])).then_inc(cmp_loaded, 16)
            with sp.Fori(0, FF_PAIRS) as j:
                load_ffn(3, j)
            s = USES0[NSA_PHASE]
            for c in range(2):
                load(c, s[c], [(in_view(staged[c][:]),
                                nsa_w_in[:, :, NSA_KV0 + c * NSA_HKV:NSA_KV0 + (c + 1) * NSA_HKV])])
            load(2, s[2], [(staged[2][:, 0:D_TILES * N_GATES].rearrange("p (k c) -> p k c", k=D_TILES),
                            nsa_w_in[:, :, NSA_GATE0:NSA_GATE0 + N_GATES])])
            with sp.Fori(0, NSA_GROUPS) as g:
                load_nsa(g, [n + 1 for n in s])
            load_ffn(5, 0, QUARTERS)
            with sp.Fori(1, FF_PAIRS) as j:
                load_ffn(5, j)
            for n in range(2 * TOK_TILES):
                sp.wait_ge(y_copied[n % 2], n // 2 + 1)
                a, half = n // 2, n % 2
                sp.dma_start(t["out"][0, a * P:(a + 1) * P, half * SEQ:(half + 1) * SEQ],
                             x_tok[:, a, half * SEQ:(half + 1) * SEQ]).then_inc(stored, 16)
            sp.wait_ge(stored, 16 * 2 * TOK_TILES)

        def loaded_value(slot, use, group=None):
            if slot == 1 and group is not None:
                return (USES0[NSA_PHASE][1] + 1) * 16 + group * 16 * QUARTERS + 16 * QUARTERS
            return use * 16 + 16

        def copy_windows(eng, copy, c, i):
            b = bank[2 * c + i]
            for g in (2 * i, 2 * i + 1):
                r = slice(g % 2 * NSA_DH, g % 2 * NSA_DH + NSA_DH)
                copy(c_t[0:NSA_DH, g, :], b[r, :]).then_inc(ct_copied, 1)
                copy(c_t[NSA_DH:P, g, 0:SEQ - 1], b[r, 1:SEQ]).then_inc(ct_copied, 1)

        @block.tensor
        def _(pe):
            def products(out, l_hi, l_lo, r_hi, r_lo, first, last):
                pe.matmul(out, l_hi, r_hi, start=first, stop=False)
                pe.matmul(out, l_hi, r_lo, start=False, stop=False)
                return pe.matmul(out, l_lo, r_hi, start=False, stop=last)

            def project_pair(slot, banks, ready, need_u=None):
                hi, lo = in_view(w_hi[slot][:]), in_view(w_lo[slot][:])
                for i, b in enumerate(banks):
                    for k in range(D_TILES):
                        if need_u is not None and i == 0:
                            pe.wait_ge(u_ready, need_u + k + 1)
                        m = products(b[:], hi[:, k, i * P:(i + 1) * P], lo[:, k, i * P:(i + 1) * P],
                                     u_hi[:, k, :], u_lo[:, k, :], k == 0, k == D_TILES - 1)
                    if i == 0:
                        m.then_inc(ready, 1)
                m.then_inc(unit_used[slot], 1)

            def spread_rstd(q, wait_sums):
                pe.wait_ge(sq_summed, wait_sums)
                for a in range(TOK_TILES):
                    m = pe.matmul(bank[6][:, a:a + 1], sq_sum[:, a * P:(a + 1) * P], ones[:, 0:1],
                                  start=True, stop=True)
                m.then_inc(sumsq_ready, 1)
                pe.wait_ge(rstd_ready, q + 1)
                for a in range(TOK_TILES):
                    m = pe.matmul(bank[7][:, a * P:(a + 1) * P], rstd[:, a:a + 1].to_broadcast([P, P]), ident[:],
                                  start=True, stop=True)
                m.then_inc(rstd_spread, 1)

            def norm(m):
                if m == 0:
                    pe.wait_ge(h_added, D_TILES)
                spread_rstd(norms_before(m), sums_before(m) + D_TILES - 1)

            def ffn_in(ph, j, need_u=None):
                s, f = USES0[ph], 2 * FF_PAIRS * FFN_NO[ph]
                for slot, banks, ready, free in ((0, bank[0:2], a_ready, silu_ready), (1, bank[2:4], b_ready, hid_ready)):
                    pe.wait_ge(split_lo[slot], s[slot] + j + 1)
                    if need_u is None:
                        pe.wait_ge(free, f + j * 2)
                    project_pair(slot, banks, ready, need_u if slot == 0 else None)

            def ffn_out(ph, i):
                s, f = USES0[ph], 2 * FF_PAIRS * FFN_NO[ph]
                hi, lo = out_view(w_hi[2][:]), out_view(w_lo[2][:])
                pe.wait_ge(split_lo[2], s[2] + i + 1)
                pe.wait_ge(mid_ready, f + i * 2 + 2)
                for d in range(D_TILES):
                    pe.wait_ge(h_added, OUT0[ph] + D_TILES + i * D_TILES + (d - 3))
                    for k in range(2):
                        m = products(bank[4 + d % 4][:], hi[:, k, d * P:(d + 1) * P], lo[:, k, d * P:(d + 1) * P],
                                     mid_hi[:, k, :], mid_lo[:, k, :], k == 0, k == 1)
                    m.then_inc(out_ready if d < D_TILES - 1 else unit_used[2], 1)

            def ffn(ph):
                ffn_in(ph, 0, need_u=D_TILES * ph)
                with pe.Fori(1, FF_PAIRS) as j:
                    ffn_in(ph, j)
                    ffn_out(ph, j - 1)
                ffn_out(ph, FF_PAIRS - 1)

            def retention_head(hd):
                s = USES0[RET_PHASE]
                before = OUT0[RET_PHASE] + D_TILES + hd * D_TILES
                for n in range(2):
                    pe.wait_ge(split_lo[n], s[n] + hd * 3 + 1)
                    if n == 0:
                        pe.wait_ge(u_ready, D_TILES * (RET_PHASE + 1))
                        pe.wait_ge(h_added, before)
                    project_pair(n, bank[2 * n:2 * n + 2], qk_ready)
                for n, slot, use in ((0, 2, s[2] + hd * 2), (1, 0, s[0] + hd * 3 + 1)):
                    hi, lo = v_view(w_hi[slot][:]), v_view(w_lo[slot][:])
                    pe.wait_ge(split_lo[slot], use + 1)
                    for a in range(TOK_TILES):
                        for k in range(4):
                            d = 4 * n + k
                            m = products(bank[4 + a][:], u_hi[:, d, a * P:(a + 1) * P], u_lo[:, d, a * P:(a + 1) * P],
                                         hi[:, k, :], lo[:, k, :], d == 0, d == D_TILES - 1)
                        if n == 1 and a < TOK_TILES - 1:
                            m.then_inc(v_ready, 1)
                    m.then_inc(unit_used[slot], 1)
                pe.wait_ge(rotated, hd * 4 + 4)
                for jb in range(TOK_TILES):
                    for c in range(2):
                        m = pe.matmul(bank[jb][:, 0:SEQ - jb * P], r_k[:, c, jb * P:(jb + 1) * P],
                                      r_q[:, c, jb * P:SEQ], start=c == 0, stop=c == 1)
                    m.then_inc(scores_ready, 1)
                for n, slot, use in ((0, 1, s[1] + hd * 3 + 1), (1, 2, s[2] + hd * 2 + 1)):
                    pe.wait_ge(split_lo[slot], use + 1)
                    pe.wait_ge(v_copied, hd * 4 + 2 * n + 2)
                    project_pair(slot, bank[4 + 2 * n:6 + 2 * n], g_ready)
                pe.wait_ge(v_copied, hd * 4 + 4)
                pe.wait_ge(decayed, hd * 4 + 4)
                for e in range(RET_E_TILES):
                    for jb in range(TOK_TILES):
                        m = pe.matmul(bank[e][:, jb * P:SEQ], r_v[:, jb, e * P:(e + 1) * P],
                                      r_p[:, r_p_at[jb]:r_p_at[jb] + SEQ - jb * P],
                                      start=jb == 0, stop=jb == TOK_TILES - 1)
                    m.then_inc(o_ready, 1)
                pe.wait_ge(silu_g_ready, hd * 4 + 4)
                spread_rstd(hd + 2, (D_TILES - 1) * 2 + (hd + 1) * (RET_E_TILES - 1))
                pe.wait_ge(z_ready, hd * 4 + 4)
                for n in range(2):
                    hi, lo = out_view(w_hi[n][:]), out_view(w_lo[n][:])
                    pe.wait_ge(split_lo[n], s[n] + hd * 3 + 3)
                    for d in range(D_TILES):
                        for k in range(2):
                            m = products(bank[d][:], hi[:, k, d * P:(d + 1) * P], lo[:, k, d * P:(d + 1) * P],
                                         mid_hi[:, 2 * n + k, :], mid_lo[:, 2 * n + k, :],
                                         n == 0 and k == 0, n == 1 and k == 1)
                        if n == 1 and d < D_TILES - 1:
                            m.then_inc(out_ready, 1)
                    m.then_inc(unit_used[n], 1)

            def compression():
                s = USES0[NSA_PHASE]
                for c in range(2):
                    pe.wait_ge(split_lo[c], s[c] + 1)
                    if c == 0:
                        pe.wait_ge(u_ready, D_TILES * (NSA_PHASE + 1))
                    project_pair(c, bank[2 * c:2 * c + 2], ct_ready)
                hi = w_hi[2][:, 0:D_TILES * N_GATES].rearrange("p (k c) -> p k c", k=D_TILES)
                lo = w_lo[2][:, 0:D_TILES * N_GATES].rearrange("p (k c) -> p k c", k=D_TILES)
                pe.wait_ge(split_lo[2], s[2] + 1)
                for a in range(TOK_TILES):
                    for k in range(D_TILES):
                        m = products(bank[4][:, a * N_GATES:(a + 1) * N_GATES], u_hi[:, k, a * P:(a + 1) * P],
                                     u_lo[:, k, a * P:(a + 1) * P], hi[:, k, :], lo[:, k, :],
                                     k == 0, k == D_TILES - 1)
                m.then_inc(unit_used[2], 1)
                for c in range(2):
                    pe.wait_ge(cmp_loaded, 32)
                    pe.wait_ge(cx_ready, CMP_K_TILES * (c + 1))
                    for m2 in range(2):
                        for kk in range(CMP_K_TILES):
                            m = pe.matmul(bank[5 + c][:, m2 * P:m2 * P + NSA_GROUPS * N_CMP],
                                          c_w1[:, c, kk, m2 * P:(m2 + 1) * P],
                                          c_x[:, kk, :, :].rearrange("p g n -> p (g n)"),
                                          start=kk == 0, stop=kk == CMP_K_TILES - 1)
                    m.then_inc(chid_ready, 1)
                    pe.wait_ge(chid_silu, c + 1)
                    if c == 0:
                        for m2 in range(2):
                            m = pe.matmul(bank[7][:, 0:NSA_GROUPS * N_CMP], c_w2[:, 0, m2, :], c_hid[:, m2, :],
                                          start=m2 == 0, stop=m2 == 1)
                        m.then_inc(ckv_ready, 1)
                    else:
                        pe.wait_ge(ckv_copied, 1)
                        for g in range(NSA_GROUPS):
                            for m2 in range(2):
                                m = pe.matmul(bank[7][0:N_CMP, g * NSA_DH:(g + 1) * NSA_DH],
                                              c_hid[:, m2, g * N_CMP:(g + 1) * N_CMP], c_w2[:, 1, m2, 0:NSA_DH],
                                              start=m2 == 0, stop=m2 == 1)
                        m.then_inc(ckv_ready, 1)

            def nsa_group(g):
                s = USES0[NSA_PHASE]
                pe.wait_ge(split_lo[0], s[0] + g + 2)
                pe.wait_ge(h_added, OUT0[NSA_PHASE] + D_TILES + g * D_TILES)
                project_pair(0, bank[0:2], gq_ready)
                hi, lo = in_view(w_hi[1][:]), in_view(w_lo[1][:])
                pe.wait_ge(split_lo[1], s[1] + g + 2)
                for k in range(D_TILES):
                    m = products(bank[2][:], hi[:, k, 0:P], lo[:, k, 0:P], u_hi[:, k, :], u_lo[:, k, :],
                                 k == 0, k == D_TILES - 1)
                m.then_inc(gk_ready, 1)
                pe.wait_ge(gq_copied, g * 2 + 2)
                pe.wait_ge(halves_zeroed, 4)
                pe.wait_ge(const_derived, 3)
                pe.wait_ge(group_set, g * GROUP_SETS + GROUP_SETS)
                for par in range(2):
                    for n in range(8):
                        pair, ib = n // TOK_TILES, n % TOK_TILES
                        m = pe.matmul(bank[4 + par][:, n * CMP_PAD:(n + 1) * CMP_PAD],
                                      n_q[:, pair, ib * P:(ib + 1) * P], c_kg[:, par, :], start=True, stop=True)
                m.then_inc(cs_ready, 1)
                for a in range(TOK_TILES):
                    for k in range(D_TILES):
                        m = products(bank[3][:, a * P:(a + 1) * P], u_hi[:, k, a * P:(a + 1) * P],
                                     u_lo[:, k, a * P:(a + 1) * P], hi[:, k, P:2 * P], lo[:, k, P:2 * P],
                                     k == 0, k == D_TILES - 1)
                m.then_inc(unit_used[1], 1)
                pe.wait_ge(gk_copied, g * 4 + 4)

                def scores(n):
                    pair, ib, par, br = ITEMS[n]
                    if n == 3:
                        pe.wait_ge(gv_copied, g + 1)
                    if n >= 4:
                        pe.wait_ge(s_exp, g * N_ITEMS + (n - 3))
                    b = bank[n % 4]
                    pe.matmul(b[:, 0:width(ib)], n_q[:, pair, ib * P:(ib + 1) * P],
                              n_k[:, br, par, 0:width(ib)], start=True, stop=False)
                    pe.matmul(b[:, ib * P:(ib + 1) * P], ident_bf[:], causal_neg_bf[:],
                              start=False, stop=True).then_inc(s_ready, 1)

                def turn(n):
                    pair, ib, par, br = ITEMS[n]
                    pe.wait_ge(p_ready, g * N_ITEMS + (n + 1))
                    if n >= 2:
                        pe.wait_ge(pt_copied[n % 2], g * (N_ITEMS // 2) + n // 2)
                    elif n == 1:
                        pe.wait_ge(cpt_copied, g + 1)
                    for jb in range(ib + 1):
                        m = pe.transpose(bank[4 + n % 2][:, jb * P:(jb + 1) * P], n_p[:, n % 3, jb * P:(jb + 1) * P],
                                         ident[:])
                    m.then_inc(pt_ready, 1)

                def values(n):
                    pair, ib, par, br = ITEMS[n]
                    half = slice(NSA_DH * (1 - par), NSA_DH * (1 - par) + P)
                    o = bank[6 + pair][:, ib * P:(ib + 1) * P]
                    pe.wait_ge(pt_copied[n % 2], g * (N_ITEMS // 2) + (n // 2 + 1))
                    if n == 0:
                        pe.wait_ge(gv_copied, g + 1)
                    for jb in range(ib + 1):
                        m = pe.matmul(o, n_v[:, jb, br, half], n_pt[:, n % 2, jb * P:(jb + 1) * P],
                                      start=par == 0 and br == 0 and jb == 0, stop=False)
                    m.then_inc(pv_done, 1)
                    if br == 1:
                        if n == 1:
                            pe.wait_ge(cpt_copied, g + 1)
                        m = pe.matmul(o, c_vg[:, ib, half], c_pt[:, par * 2 + pair, :], start=False, stop=par == 1)
                        if ib == TOK_TILES - 1 and par == 1:
                            m.then_inc(no_ready, 1)

                scores(0)
                scores(1)
                pe.wait_ge(cs_steps, g * CS_STEPS + CS_STEPS)
                for i in range(NSA_HPG):
                    m = pe.transpose(bank[5][:, i * P:(i + 1) * P],
                                     c_p[:, i * TOK_TILES:(i + 1) * TOK_TILES, :].rearrange("p i n -> p (i n)"),
                                     ident[:])
                m.then_inc(cpt_ready, 1)
                for n in range(N_ITEMS + 1):
                    if n + 2 < N_ITEMS:
                        scores(n + 2)
                    if n < N_ITEMS:
                        turn(n)
                    if n >= 1:
                        values(n - 1)
                pe.wait_ge(no_split, g * 2 + 2)
                pe.wait_ge(split_lo[2], s[2] + g + 2)
                hi, lo = out_view(w_hi[2][:]), out_view(w_lo[2][:])
                for d in range(D_TILES):
                    if d >= 4:
                        pe.wait_ge(h_added, OUT0[NSA_PHASE] + D_TILES + g * D_TILES + (d - 3))
                    for k in range(2):
                        m = products(bank[d % 4][:], hi[:, k, d * P:(d + 1) * P], lo[:, k, d * P:(d + 1) * P],
                                     mid_hi[:, k, :], mid_lo[:, k, :], k == 0, k == 1)
                    m.then_inc(out_ready if d < D_TILES - 1 else unit_used[2], 1)

            pe.wait_ge(const_set, 4)
            pe.wait_ge(const_loaded, 16 * N_CONST_LOADS)
            pe.transpose(bank[7][:, 0:N_ROWS], rows[:], ident[0:N_ROWS, 0:N_ROWS]).then_inc(rows_turned, 1)
            for d in range(D_TILES):
                if d == D_TILES - 1:
                    pe.wait_ge(cols_ready, 1)
                for a in range(TOK_TILES):
                    pe.wait_ge(x_loaded, 16 * TOK_TILES)
                    m = pe.transpose(bank[d][:, a * P:(a + 1) * P], x_tok[:, a, d * P:(d + 1) * P], ident[:])
                m.then_inc(x_turned, 1)
            norm(0)
            ffn(0)
            norm(1)
            with pe.Fori(0, RET_HEADS) as hd:
                retention_head(hd)
            norm(2)
            ffn(2)
            norm(3)
            ffn(3)
            norm(4)
            compression()
            with pe.Fori(0, NSA_GROUPS) as g:
                nsa_group(g)
            norm(5)
            ffn(5)
            norm(6)
            pe.wait_ge(y_ready, D_TILES)
            for n in range(2 * TOK_TILES):
                a, half = n // 2, n % 2
                for i in range(4):
                    m = pe.transpose(bank[n][:, i * P:(i + 1) * P], y[:, 4 * half + i, a * P:(a + 1) * P], ident[:])
                m.then_inc(y_turned, 1)

        @block.scalar
        def _(act):
            def split(slot, use, value=None):
                act.wait_ge(loaded[slot], loaded_value(slot, use) if value is None else value)
                if not isinstance(use, int) or use > 0:
                    act.wait_ge(unit_used[slot], use)
                act.activation(w_hi[slot][:], staged[slot][:], ACT.Copy).then_inc(split_hi[slot], 1)

            def root(q, n_features):
                act.wait_ge(sumsq_ready, q + 1)
                act.activation(std[:], bank[6][:, 0:TOK_TILES], ACT.Sqrt, bias=eps[:], scale=1.0 / n_features)\
                   .then_inc(std_ready, 1)

            def norm(m):
                for d in range(D_TILES):
                    act.wait_ge(h_added, OUT0[m] + d + 1)
                    if d >= 3:
                        act.wait_ge(sq_summed, sums_before(m) + d - 2)
                    act.activation(sq_sum[:] if d == 0 else sq[:, d % 2, :], h[:, d, :], ACT.Square)\
                       .then_inc(squared, 1)
                root(norms_before(m), D_MODEL)
                if m < N_PHASES:
                    for d in range(D_TILES):
                        act.wait_ge(u_scaled, D_TILES * m + d + 1)
                        act.activation(u_hi[:, d, :], u_f32[:, d % 3, :], ACT.Copy).then_inc(u_hi_ready, 1)

            def ffn_pair(ph, j, more=True):
                s, no = USES0[ph], FF_PAIRS * FFN_NO[ph]
                later = ph == N_PHASES - 1
                for i in range(2):
                    if i == 0:
                        act.wait_ge(a_ready, no + j + 1)
                    else:
                        act.wait_ge(unit_used[0], s[0] + j + 1)
                    if ph > 0 or not isinstance(j, int) or j > 0:
                        act.wait_ge(hid_ready, 2 * no - 1 + i + j * 2)
                    act.activation(silu_a[:, i, :], bank[i][:], ACT.Silu).then_inc(silu_ready, 1)
                if more:
                    split(0, s[0] + j + 1)
                    split(1, s[1] + j + 1, value=(s[1] + QUARTERS + 1) * 16 + j * 16 + 48 * NSA_GROUPS if later else None)
                for i in range(2):
                    act.wait_ge(hid_ready, 2 * no + 1 + i + j * 2)
                    if i == 0 and (ph > 0 or not isinstance(j, int) or j > 0):
                        act.wait_ge(unit_used[2], s[2] + j)
                    act.activation(mid_hi[:, i, :], hid[:, i, :], ACT.Copy).then_inc(mid_hi_ready, 1)
                split(2, s[2] + j)

            def ffn(ph):
                ffn_pair(ph, 0)
                last = ph == N_PHASES - 1
                with act.Fori(1, FF_PAIRS - (1 if last else 0)) as j:
                    ffn_pair(ph, j)
                if last:
                    ffn_pair(ph, FF_PAIRS - 1, more=False)

            def retention_head(hd):
                s = USES0[RET_PHASE]
                split(2, s[2] + hd * 2)
                split(0, s[0] + hd * 3 + 1)
                split(1, s[1] + hd * 3 + 1)
                split(2, s[2] + hd * 2 + 1)
                for a in range(TOK_TILES):
                    if a < TOK_TILES - 1:
                        act.wait_ge(v_ready, hd * 3 + a + 1)
                    else:
                        act.wait_ge(unit_used[0], s[0] + hd * 3 + 2)
                    act.activation(r_v[:, a, :], bank[4 + a][:], ACT.Copy).then_inc(v_copied, 1)
                split(0, s[0] + hd * 3 + 2)
                for e in range(RET_E_TILES):
                    if e % 2 == 0:
                        act.wait_ge(g_ready, hd * 2 + e // 2 + 1)
                    elif e == 1:
                        act.wait_ge(unit_used[1], s[1] + hd * 3 + 2)
                    else:
                        act.wait_ge(unit_used[2], s[2] + hd * 2 + 2)
                    act.wait_ge(gated, hd * 4)
                    act.activation(r_silu_g[:, e, :], bank[4 + e][:], ACT.Silu).then_inc(silu_g_ready, 1)
                    if e == 1:
                        split(1, s[1] + hd * 3 + 2)
                for e in range(RET_E_TILES):
                    act.wait_ge(o_ready, hd * 4 + e + 1)
                    if e == 3:
                        act.wait_ge(sq_summed, 2 * (D_TILES - 1) + 1 + hd * 3)
                    act.activation(sq_sum[:] if e == 0 else sq[:, e % 2, :], bank[e][:], ACT.Square)\
                       .then_inc(squared, 1)
                root(hd + 2, RET_DV)
                for e in range(RET_E_TILES):
                    act.wait_ge(normed, hd * 4 + e + 1)
                    act.activation(mid_hi[:, e, :], r_og[:, e, :], ACT.Copy).then_inc(z_hi_ready, 1)
                split(0, s[0] + hd * 3 + 3)
                split(1, s[1] + hd * 3 + 3)

            def compression():
                s = USES0[NSA_PHASE]
                split(2, s[2])
                for c in range(2):
                    act.wait_ge(ct_ready, c + 1)
                    if c == 1:
                        act.wait_ge(cx_ready, CMP_K_TILES)
                    copy_windows(act, lambda o, i: act.activation(o, i, ACT.Copy), c, 0)
                    split(c, s[c] + 1, value=None if c == 0 else loaded_value(1, None, group=0))
                act.wait_ge(unit_used[2], s[2] + 1)
                act.activation(gates[:].rearrange("p a c -> p (a c)"), bank[4][:, 0:TOK_TILES * N_GATES], ACT.Sigmoid)\
                   .then_inc(gates_set, 1)
                for c in range(2):
                    act.wait_ge(chid_ready, c + 1)
                    if c == 1:
                        act.wait_ge(ckv_ready, 1)
                    act.activation(c_hid[:], bank[5 + c][:, 0:2 * P].rearrange("p (m n) -> p m n", m=2)[
                        :, :, 0:NSA_GROUPS * N_CMP], ACT.Silu).then_inc(chid_silu, 1)

            def nsa_group(g):
                s = USES0[NSA_PHASE]
                split(2, s[2] + g + 1)
                for i in range(2):
                    if i == 0:
                        act.wait_ge(gq_ready, g + 1)
                    else:
                        act.wait_ge(unit_used[0], s[0] + g + 2)
                    act.activation(n_q[:, i, :], bank[i][:], ACT.Copy).then_inc(gq_copied, 1)
                split(0, s[0] + g + 2)
                act.wait_ge(cs_steps, g * CS_STEPS + 4)
                act.activation(c_p[:].rearrange("p a n -> p (a n)"), c_s[:].rearrange("p a n -> p (a n)"), ACT.Exp,
                               scale=NSA_SCALE).then_inc(cs_exp, 1)
                act.wait_ge(unit_used[1], s[1] + g + 2)
                act.wait_ge(halves_zeroed, 4)
                act.activation(n_v[:, :, :, NSA_DH:2 * NSA_DH], bank[3][:].rearrange("p (a b d) -> p a b d", a=TOK_TILES, b=2),
                               ACT.Copy).then_inc(gv_copied, 1)
                split(1, s[1] + g + 2, value=loaded_value(1, None, group=g + 1))

                def turned(n):
                    pair, ib, par, br = ITEMS[n]
                    act.wait_ge(pt_ready, g * N_ITEMS + (n + 1))
                    if n >= 2:
                        act.wait_ge(pv_done, g * N_ITEMS + (n - 1))
                    act.activation(n_pt[:, 0, 0:width(ib)], bank[4][:, 0:width(ib)], ACT.Copy).then_inc(pt_copied[0], 1)

                def o_hi(i):
                    act.wait_ge(no_ready, g * 2 + (i + 1))
                    act.activation(mid_hi[:, i, :], bank[6 + i][:], ACT.Copy).then_inc(no_hi_ready, 1)

                for n in range(N_ITEMS + 2):
                    if n < N_ITEMS:
                        pair, ib, par, br = ITEMS[n]
                        act.wait_ge(s_biased, g * N_ITEMS + (n + 1))
                        if n >= 3:
                            act.wait_ge(pt_ready, g * N_ITEMS + (n - 2))
                        act.activation(n_p[:, n % 3, 0:width(ib)], bank[n % 4][:, 0:width(ib)], ACT.Exp,
                                       bias=s_bias[:, n % 4:n % 4 + 1], scale=NSA_SCALE,
                                       accum_out=s_den[:, n % 4:n % 4 + 1]).then_inc(s_exp, 1)
                    if n == 1:
                        act.wait_ge(cpt_ready, g + 1)
                        act.activation(c_pt[:].rearrange("p a q -> p (a q)"), bank[5][:], ACT.Copy)\
                           .then_inc(cpt_copied, 1)
                    if n >= 2 and n % 2 == 0:
                        turned(n - 2)
                    if n == N_ITEMS // 2 + 3:
                        o_hi(0)
                o_hi(1)

            split(0, 0)
            split(1, 0)
            norm(0)
            ffn(0)
            norm(1)
            with act.Fori(0, RET_HEADS) as hd:
                retention_head(hd)
            norm(2)
            ffn(2)
            norm(3)
            ffn(3)
            norm(4)
            compression()
            with act.Fori(0, NSA_GROUPS) as g:
                nsa_group(g)
            norm(5)
            ffn(5)
            norm(6)
            for n in range(0, 2 * TOK_TILES, 2):
                act.wait_ge(y_turned, n + 1)
                act.activation(x_tok[:, n // 2, 0:SEQ], bank[n][:], ACT.Copy).then_inc(y_copied[0], 1)

        @block.vector
        def _(dve):
            def split(slot, use, words=UNIT):
                dve.wait_ge(split_hi[slot], use + 1)
                dve.tensor_tensor(w_lo[slot][:], staged[slot][:], w_hi[slot][:].bitcast(F32), ALU.subtract)\
                   .then_inc(split_lo[slot], 1)

            def norm(m):
                q = norms_before(m)
                for d in range(1, D_TILES):
                    dve.wait_ge(squared, squares_before(m) + d + 1)
                    if d > 1:
                        dve.wait_ge(sq_summed, sums_before(m) + d - 1)
                    dve.tensor_tensor(sq_sum[:], sq_sum[:], sq[:, d % 2, :], ALU.add).then_inc(sq_summed, 1)
                dve.wait_ge(std_ready, q + 1)
                dve.reciprocal(rstd[:], std[:]).then_inc(rstd_ready, 1)
                dve.wait_ge(rstd_spread, q + 1)
                last = m == N_PHASES

                def low(d):
                    dve.wait_ge(u_hi_ready, D_TILES * m + d + 1)
                    dve.tensor_tensor(u_lo[:, d, :], u_f32[:, d % 3, :], u_hi[:, d, :].bitcast(F32), ALU.subtract)\
                       .then_inc(u_ready, 1)

                for d in range(D_TILES):
                    gain = cols[:, ROW_NORM[m] + d:ROW_NORM[m] + d + 1]
                    if not last and D_TILES * m + max(d - 2, 0) > 0:
                        dve.wait_ge(u_ready, D_TILES * m + max(d - 2, 0))
                    dve.scalar_tensor_tensor(out=y[:, d, :] if last else u_f32[:, d % 3, :], in0=h[:, d, :], scalar=gain,
                                             in1=bank[7][:], op0=ALU.mult, op1=ALU.mult)\
                       .then_inc(y_ready if last else u_scaled, 1)
                    if d >= 1 and not last:
                        low(d - 1)
                if not last:
                    low(D_TILES - 1)

            def add_out(ph, group, banks, slot, use, scale):
                for d in range(D_TILES):
                    if d < D_TILES - 1:
                        dve.wait_ge(out_ready, OUT_READY0[ph] + d + 1 + group * (D_TILES - 1))
                    else:
                        dve.wait_ge(unit_used[slot], use + 1)
                    dve.wait_ge(h_added, OUT0[ph] + d + 1 + group * D_TILES)
                    dve.scalar_tensor_tensor(out=h[:, d, :], in0=banks(d)[:], scalar=scale, in1=h[:, d, :],
                                             op0=ALU.mult, op1=ALU.add).then_inc(h_added, 1)

            def ffn_pair(ph, j, more=True, before=True):
                s, no = USES0[ph], FF_PAIRS * FFN_NO[ph]
                if more:
                    split(0, s[0] + j + 1)
                if ph > 0 or not isinstance(j, int) or j > 0:
                    dve.wait_ge(mid_ready, 2 * no + j * 2)
                for i in range(2):
                    dve.wait_ge(silu_ready, 2 * no + 1 + i + j * 2)
                    if i == 0:
                        dve.wait_ge(b_ready, no + j + 1)
                    else:
                        dve.wait_ge(unit_used[1], s[1] + j + 1)
                    dve.tensor_tensor(hid[:, i, :], silu_a[:, i, :], bank[2 + i][:], ALU.mult).then_inc(hid_ready, 1)
                if more:
                    split(1, s[1] + j + 1)
                if before:
                    ffn_out(ph, j - 1)
                for i in range(2):
                    dve.wait_ge(mid_hi_ready, 2 * no + 1 + i + j * 2)
                    dve.tensor_tensor(mid_lo[:, i, :], hid[:, i, :], mid_hi[:, i, :].bitcast(F32), ALU.subtract)\
                       .then_inc(mid_ready, 1)
                split(2, s[2] + j)

            def ffn_out(ph, i):
                add_out(ph, i, lambda d: bank[4 + d % 4], 2, USES0[ph][2] + i, 0.5)

            def ffn(ph):
                ffn_pair(ph, 0, before=False)
                last = ph == N_PHASES - 1
                with dve.Fori(1, FF_PAIRS - (1 if last else 0)) as j:
                    ffn_pair(ph, j)
                if last:
                    ffn_pair(ph, FF_PAIRS - 1, more=False)
                ffn_out(ph, FF_PAIRS - 1)

            def retention_head(hd):
                s = USES0[RET_PHASE]

                def rotate(n, x, dst):
                    prods = ((0, x[0], cos_t), (1, x[1], sin_t), (2, x[0], sin_t), (3, x[1], cos_t))
                    dve.wait_ge(qk_ready, hd * 2 + n + 1)
                    dve.wait_ge(unit_used[n], s[n] + hd * 3 + 1)
                    dve.wait_ge(ret_loaded, 48)
                    if n == 0:
                        dve.wait_ge(z_ready, hd * 4)
                    else:
                        dve.wait_ge(rotated, hd * 4 + 2)
                    for i, b, table in prods:
                        dve.tensor_tensor(r_og[:, i, :], b[:], table, ALU.mult).then_inc(rot_products, 1)
                    dve.wait_ge(rot_products, hd * 8 + 4 * n + 4)
                    dve.tensor_tensor(dst[:, 0, :], r_og[:, 0, :], r_og[:, 1, :], ALU.subtract).then_inc(rotated, 1)
                    dve.tensor_tensor(dst[:, 1, :], r_og[:, 2, :], r_og[:, 3, :], ALU.add).then_inc(rotated, 1)

                split(2, s[2] + hd * 2)
                rotate(0, bank[0:2], r_q)
                split(0, s[0] + hd * 3 + 1)
                rotate(1, bank[2:4], r_k)
                split(1, s[1] + hd * 3 + 1)
                split(2, s[2] + hd * 2 + 1)
                for jb in range(TOK_TILES):
                    n = SEQ - jb * P
                    dve.wait_ge(scores_ready, hd * 4 + jb + 1)
                    dve.tensor_tensor(r_p[:, r_p_at[jb]:r_p_at[jb] + n], bank[jb][:, 0:n], decay[:, ds(hd * SEQ, n)],
                                      ALU.mult).then_inc(decayed, 1)
                split(0, s[0] + hd * 3 + 2)
                split(1, s[1] + hd * 3 + 2)
                squares = 2 * D_TILES + hd * RET_E_TILES
                sums = 2 * (D_TILES - 1) + hd * (RET_E_TILES - 1)
                for e in range(RET_E_TILES):
                    dve.wait_ge(squared, squares + e + 1)
                    if e >= 1:
                        dve.wait_ge(sq_summed, sums + e - 1)
                        dve.tensor_tensor(sq_sum[:], sq_sum[:], sq[:, e % 2, :], ALU.add).then_inc(sq_summed, 1)
                for e in range(RET_E_TILES):
                    dve.wait_ge(silu_g_ready, hd * 4 + e + 1)
                    dve.scalar_tensor_tensor(out=r_og[:, e, :], in0=bank[e][:], scalar=cols[:, ds(hd * 4 + (ROW_GN + e), 1)],
                                             in1=r_silu_g[:, e, :], op0=ALU.mult, op1=ALU.mult).then_inc(gated, 1)
                dve.wait_ge(std_ready, hd + 3)
                dve.reciprocal(rstd[:], std[:]).then_inc(rstd_ready, 1)
                dve.wait_ge(rstd_spread, hd + 3)
                for e in range(RET_E_TILES + 1):
                    if e < RET_E_TILES:
                        dve.wait_ge(gated, hd * 4 + e + 1)
                        dve.tensor_tensor(r_og[:, e, :], r_og[:, e, :], bank[7][:], ALU.mult).then_inc(normed, 1)
                    if e >= 1:
                        dve.wait_ge(z_hi_ready, hd * 4 + e)
                        dve.tensor_tensor(mid_lo[:, e - 1, :], r_og[:, e - 1, :], mid_hi[:, e - 1, :].bitcast(F32),
                                          ALU.subtract).then_inc(z_ready, 1)
                split(0, s[0] + hd * 3 + 3)
                add_out(RET_PHASE, hd, lambda d: bank[d], 1, s[1] + hd * 3 + 2, 1.0)
                split(1, s[1] + hd * 3 + 3)

            def compression():
                s = USES0[NSA_PHASE]
                split(2, s[2])
                for c in range(2):
                    dve.wait_ge(unit_used[c], s[c] + 1)
                    if c == 1:
                        dve.wait_ge(cx_ready, CMP_K_TILES)
                    copy_windows(dve, dve.tensor_copy, c, 1)
                    dve.wait_ge(ct_copied, 8 * (c + 1))
                    if c == 1:
                        dve.wait_ge(chid_ready, 1)
                    for kk in range(CMP_K_TILES):
                        col = ROW_POS + c * CMP_K_TILES + kk
                        dve.tensor_scalar(c_x[:, kk, :, :], c_t[:, :, 2 * kk:2 * kk + CMP_STRIDE * (N_CMP - 1) + 1:CMP_STRIDE],
                                          cols[:, col:col + 1], None, ALU.add).then_inc(cx_ready, 1)
                    split(c, s[c] + 1)
                dve.wait_ge(const_set, 4)
                dve.wait_ge(ckv_ready, 1)
                dve.tensor_copy(c_k[:, :, 0:N_CMP], bank[7][:, 0:NSA_GROUPS * N_CMP].rearrange("p (g n) -> p g n", g=NSA_GROUPS))\
                   .then_inc(ckv_copied, 1)
                dve.wait_ge(ckv_ready, 2)
                dve.tensor_copy(c_v[0:N_CMP, :, :],
                                bank[7][0:N_CMP, 0:NSA_GROUPS * NSA_DH].rearrange("p (g d) -> p g d", g=NSA_GROUPS))\
                   .then_inc(ckv_copied, 1)

            def nsa_group(g):
                s = USES0[NSA_PHASE]
                split(2, s[2] + g + 1)
                dve.wait_ge(halves_zeroed, 4)
                dve.wait_ge(const_derived, 3)
                dve.wait_ge(ckv_copied, 2)
                dve.wait_ge(gates_set, 1)
                for par in range(2):
                    r = slice(par * NSA_DH, (par + 1) * NSA_DH)
                    dve.tensor_copy(c_kg[r, par, :], c_k[r, ds(g, 1), :].rearrange("p a n -> p (a n)")).then_inc(group_set, 1)
                for ib in range(TOK_TILES):
                    dve.tensor_copy(c_vg[ib * CMP_PAD:(ib + 1) * CMP_PAD, ib, NSA_DH:2 * NSA_DH],
                                    c_v[:, ds(g, 1), :].rearrange("p a n -> p (a n)")).then_inc(group_set, 1)
                for br in range(3):
                    dve.tensor_copy(gate_g[:, br, :].rearrange("p (b a i) -> p b a i", b=2, a=2),
                                    gates[:, :, ds(g * NSA_HPG + br * NSA_HEADS, NSA_HPG)]
                                    .rearrange("p i (a b) -> p b a i", b=2)).then_inc(group_set, 1)
                dve.wait_ge(gk_ready, g + 1)
                for br in range(2):
                    for par in range(2):
                        dve.tensor_copy(n_k[par * NSA_DH:(par + 1) * NSA_DH, br, par, :],
                                        bank[2][br * NSA_DH:(br + 1) * NSA_DH, :]).then_inc(gk_copied, 1)

                steps = g * CS_STEPS

                def flat(v):
                    return v.rearrange("p a n -> p (a n)")

                def over_keys(v):
                    return v.unsqueeze(2).to_broadcast([P, 16, CMP_PAD])

                dve.wait_ge(cs_ready, g + 1)
                by_head = "p (r i) n -> p r (i n)"
                for par in range(2):
                    dve.tensor_tensor(c_s[:, 8 * par:8 * par + 8, :].rearrange(by_head, r=2),
                                      bank[4 + par][:, 0:2 * P].rearrange("p (r m) -> p r m", r=2),
                                      flat(cmp_neg[:]).unsqueeze(1).to_broadcast([P, 2, P]), ALU.add).then_inc(cs_steps, 1)
                dve.wait_ge(cs_steps, steps + 2)
                dve.reduce_max(c_max, c_s, AX_X).then_inc(cs_steps, 1)
                dve.wait_ge(cs_steps, steps + 3)
                dve.tensor_tensor(c_s, c_s, over_keys(c_max), ALU.subtract).then_inc(cs_steps, 1)
                dve.wait_ge(cs_exp, g + 1)
                dve.tensor_tensor(c_p[:].rearrange(by_head, r=4), c_p[:].rearrange(by_head, r=4),
                                  flat(cmp_mask[:]).unsqueeze(1).to_broadcast([P, 4, P]), ALU.mult).then_inc(cs_steps, 1)
                dve.wait_ge(cs_steps, steps + 5)
                dve.reduce_sum(c_den, c_p, AX_X).then_inc(cs_steps, 1)
                dve.wait_ge(cs_steps, steps + 6)
                dve.tensor_scalar(c_den, c_den, 1e-30, None, ALU.max).then_inc(cs_steps, 1)
                dve.wait_ge(cs_steps, steps + 7)
                dve.reciprocal(c_rden, c_den).then_inc(cs_steps, 1)
                dve.wait_ge(cs_steps, steps + 8)
                dve.wait_ge(group_set, g * GROUP_SETS + GROUP_SETS)
                dve.tensor_tensor(c_fac, c_rden, gate_g[:, 0, :], ALU.mult).then_inc(cs_steps, 1)
                dve.wait_ge(cs_steps, steps + 9)
                dve.tensor_tensor(c_p, c_p, over_keys(c_fac), ALU.mult).then_inc(cs_steps, 1)

                def largest(n):
                    pair, ib, par, br = ITEMS[n]
                    c = slice(n % 4, n % 4 + 1)
                    dve.wait_ge(s_ready, g * N_ITEMS + (n + 1))
                    dve.reduce_max(s_max[:, c], bank[n % 4][:, 0:width(ib)], AX_X).then_inc(s_maxed, 1)
                    dve.wait_ge(s_maxed, g * N_ITEMS + (n + 1))
                    dve.tensor_scalar(s_bias[:, c], s_max[:, c], -NSA_SCALE, None, ALU.mult).then_inc(s_biased, 1)

                def weigh(n):
                    pair, ib, par, br = ITEMS[n]
                    c = slice(n % 4, n % 4 + 1)
                    at = (par * 2 + pair) * TOK_TILES + ib
                    dve.wait_ge(s_exp, g * N_ITEMS + (n + 1))
                    dve.reciprocal(s_rden[:, c], s_den[:, c]).then_inc(s_recip, 1)
                    dve.wait_ge(s_recip, g * N_ITEMS + (n + 1))
                    dve.tensor_scalar(n_p[:, n % 3, 0:width(ib)], n_p[:, n % 3, 0:width(ib)], s_rden[:, c],
                                      gate_g[:, br + 1, at:at + 1], ALU.mult, ALU.mult).then_inc(p_ready, 1)

                def turned(n):
                    pair, ib, par, br = ITEMS[n]
                    dve.wait_ge(pt_ready, g * N_ITEMS + (n + 1))
                    if n >= 2:
                        dve.wait_ge(pv_done, g * N_ITEMS + (n - 1))
                    dve.tensor_copy(n_pt[:, 1, 0:width(ib)], bank[5][:, 0:width(ib)]).then_inc(pt_copied[1], 1)

                def o_lo(i):
                    dve.wait_ge(no_hi_ready, g * 2 + (i + 1))
                    dve.tensor_tensor(mid_lo[:, i, :], bank[6 + i][:], mid_hi[:, i, :].bitcast(F32), ALU.subtract)\
                       .then_inc(no_split, 1)

                largest(0)
                largest(1)
                for n in range(N_ITEMS + 1):
                    if n < N_ITEMS:
                        weigh(n)
                    if n + 2 < N_ITEMS:
                        largest(n + 2)
                    if n == 2:
                        split(0, s[0] + g + 2)
                    if n == 4:
                        split(1, s[1] + g + 2)
                    if n >= 1 and (n - 1) % 2 == 1:
                        turned(n - 1)
                    if n == N_ITEMS // 2 + 4:
                        o_lo(0)
                o_lo(1)
                add_out(NSA_PHASE, g, lambda d: bank[d % 4], 2, s[2] + g + 1, 1.0)

            dve.wait_ge(const_loaded, 16 * N_CONST_LOADS)
            dve.tensor_copy(ident_bf[:], ident[:]).then_inc(const_derived, 1)
            dve.tensor_copy(causal_neg_bf[:], causal_neg[:]).then_inc(const_derived, 1)
            dve.tensor_scalar(cmp_neg[:], cmp_mask[:], -1.0, -NEG_RAW, ALU.add, ALU.mult).then_inc(const_derived, 1)
            dve.wait_ge(rows_turned, 1)
            dve.tensor_copy(cols[:], bank[7][:, 0:N_ROWS]).then_inc(cols_ready, 1)
            for d in range(D_TILES):
                dve.wait_ge(x_turned, d + 1)
                dve.tensor_copy(h[:, d, :], bank[d][:]).then_inc(h_added, 1)
            dve.wait_ge(cols_ready, 1)
            dve.wait_ge(h_added, D_TILES)
            split(0, 0)
            split(1, 0)
            norm(0)
            ffn(0)
            norm(1)
            with dve.Fori(0, RET_HEADS) as hd:
                retention_head(hd)
            norm(2)
            ffn(2)
            norm(3)
            ffn(3)
            norm(4)
            compression()
            with dve.Fori(0, NSA_GROUPS) as g:
                nsa_group(g)
            norm(5)
            ffn(5)
            norm(6)
            for n in range(1, 2 * TOK_TILES, 2):
                dve.wait_ge(y_turned, n + 1)
                dve.tensor_copy(x_tok[:, n // 2, SEQ:2 * SEQ], bank[n][:]).then_inc(y_copied[1], 1)

        @block.gpsimd
        def _(pool):
            pool.memset(ones[:], 1.0).then_inc(const_set, 1)
            pool.memset(eps[:], NORM_EPS).then_inc(const_set, 1)
            pool.memset(c_k[:], 0.0).then_inc(const_set, 1)
            pool.memset(c_v[:], 0.0).then_inc(const_set, 1)
            pool.wait_ge(ckv_ready, 2)
            pool.memset(n_k, 0.0).then_inc(halves_zeroed, 1)
            pool.memset(n_v, 0.0).then_inc(halves_zeroed, 1)
            pool.memset(c_kg, 0.0).then_inc(halves_zeroed, 1)
            pool.memset(c_vg, 0.0).then_inc(halves_zeroed, 1)


_INS = ["x", "norm_ffn1", "ffn1_w_in", "ffn1_w_out", "norm_mix", "norm_ffn2", "ffn2_w_in", "ffn2_w_out", "norm_final",
        "ret_w_in", "ret_gn_gain", "ret_w_out",
        "nsa_w_in", "nsa_cmp_pos", "nsa_cmp_w1", "nsa_cmp_w2", "nsa_w_out"]


def shape_constants():
    half = RET_DK // 2
    inv = np.float32(10000.0) ** (-np.arange(half, dtype=np.float32) / np.float32(half))
    ang = inv.astype(np.float32)[:, None] * np.arange(SEQ, dtype=np.float32)[None, :]
    log_gamma = np.log1p(-np.exp2(-5.0 - np.arange(RET_HEADS, dtype=np.float64)))
    rel = np.arange(SEQ)[None, :] - np.arange(P)[:, None]
    decay = np.where(rel >= 0, np.exp(np.maximum(rel, 0) * log_gamma[:, None, None]), 0.0) * RET_DK ** -0.5
    q = np.arange(SEQ).reshape(TOK_TILES, P).T
    n = np.arange(CMP_PAD)
    cmp_mask = (n * CMP_STRIDE + CMP_LEN - 1 <= q[:, :, None]) & (n < N_CMP)
    causal = np.where(np.arange(P)[None, :] <= np.arange(P)[:, None], 0.0, NEG_RAW)
    return {
        "c_ident": np.eye(P, dtype=np.float32),
        "c_cos": np.cos(ang).astype(np.float32),
        "c_sin": np.sin(ang).astype(np.float32),
        "c_decay": np.ascontiguousarray(decay.transpose(1, 0, 2).reshape(P, RET_HEADS * SEQ), dtype=np.float32),
        "c_causal": causal.astype(np.float32),
        "c_cmp_mask": cmp_mask.astype(np.float32),
    }


def kernel(**inputs):
    import concourse.bacc as bacc
    from concourse.bass_utils import run_bass_kernel_spmd

    nc = bacc.Bacc("TRN2", target_bir_lowering=False, num_devices=1)
    arrays = {name: np.ascontiguousarray(inputs[name]) for name in _INS}
    arrays.update(shape_constants())
    t = {name: nc.dram_tensor("in_" + name, a.shape, mybir.dt.from_np(a.dtype), kind="ExternalInput").ap()
         for name, a in arrays.items()}
    t["out"] = nc.dram_tensor("out_y", (1, SEQ, D_MODEL), F32, kind="ExternalOutput").ap()
    build(nc, t)
    r = run_bass_kernel_spmd(nc, [{"in_" + name: a for name, a in arrays.items()}], core_ids=[0])
    return r.results[0]["out_y"]
```

```python
from contextlib import ExitStack

import numpy as np

import concourse.bass as bass
import concourse.mybir as mybir

F32 = mybir.dt.float32
F32R = mybir.dt.float32r
BF16 = mybir.dt.bfloat16
ACT = mybir.ActivationFunctionType
ALU = mybir.AluOpType
AX_X = mybir.AxisListType.X
ds = bass.ds

P = 128
SEQ = 512
D_MODEL = 1024
D_FF = 2816
NORM_EPS = 1e-6
TOK_TILES = SEQ // P
D_TILES = D_MODEL // P
UNIT = 2048
PAIR = 2 * P
FF_PAIRS = D_FF // PAIR

RET_HEADS = 4
RET_DK = D_MODEL // RET_HEADS
RET_DV = 2 * RET_DK
RET_E_TILES = RET_DV // P
RET_K0 = RET_HEADS * RET_DK
RET_V0 = 2 * RET_K0
RET_G0 = RET_V0 + RET_HEADS * RET_DV

NSA_HEADS = 16
NSA_GROUPS = 4
NSA_HPG = NSA_HEADS // NSA_GROUPS
NSA_DH = D_MODEL // NSA_HEADS
NSA_KV0 = NSA_HEADS * NSA_DH
NSA_HKV = NSA_GROUPS * NSA_DH
NSA_GATE0 = NSA_KV0 + 6 * NSA_HKV
N_GATES = 3 * NSA_HEADS
CMP_LEN = 32
CMP_STRIDE = 16
CMP_HID = 4 * NSA_DH
N_CMP = (SEQ - CMP_LEN) // CMP_STRIDE + 1
CMP_PAD = 32
CMP_K_TILES = CMP_LEN * NSA_DH // P
N_WIN = NSA_GROUPS * N_CMP
KEY_PIECES = 2
NSA_SCALE = NSA_DH ** -0.5
NEG_RAW = -1e30 / NSA_SCALE
SEL_LEN, N_SEL, WINDOW = 64, 16, 512
assert SEQ // SEL_LEN <= N_SEL and SEQ <= WINDOW

FFN_USES = (FF_PAIRS,) * 3
RET_USES = (3 * RET_HEADS, 3 * RET_HEADS, 2 * RET_HEADS)
NSA_FIRST = (3, 3, 3)
NSA_USES = tuple(n + NSA_GROUPS for n in NSA_FIRST)
PHASE_USES = [FFN_USES, RET_USES, FFN_USES, FFN_USES, NSA_USES, FFN_USES]
PHASE_OUT = [D_TILES * n for n in (FF_PAIRS, RET_HEADS, FF_PAIRS, FF_PAIRS, NSA_GROUPS, FF_PAIRS)]
N_PHASES = len(PHASE_USES)
FFN_NO = {0: 0, 2: 1, 3: 2, 5: 3}
RET_PHASE, NSA_PHASE = 1, 4
USES0 = [[sum(u[s] for u in PHASE_USES[:ph]) for s in range(3)] for ph in range(N_PHASES)]
OUT0 = [sum(PHASE_OUT[:ph]) for ph in range(N_PHASES + 1)]
OUT_READY0 = [n // D_TILES * (D_TILES - 1) for n in OUT0]

ROW_NORM = [0, 16, 32, 8, 24, 40, 48]
ROW_GN = 56
ROW_POS = 72
N_ROWS = ROW_POS + 2 * CMP_K_TILES


ITEMS = [(pair, ib, par) for pair in range(2) for ib in range(TOK_TILES) for par in range(2)]
N_ITEMS = len(ITEMS)
LATE_ITEMS = 5
BATCHES = [(pair, ib, pars) for pair in range(2) for ib in range(TOK_TILES)
           for pars in (((0, 1),) if ib < 2 else ((0,), (1,)))]
BATCH_OF = [next(b for b, (pair, ib, pars) in enumerate(BATCHES) if (pair, ib) == (i[0], i[1]) and i[2] in pars)
            for i in ITEMS]
CS_STEPS = 12
GROUP_SETS = 12
RET_OUT_BANK = (4, 5, 6, 7, 0, 1, 2, 3)
MID_SQUARES = RET_HEADS * RET_E_TILES

WORK = 9472
PARTS = 8320
V_WORDS = TOK_TILES * 2 * NSA_HKV


def batch_end(n):
    return max(i for i in range(N_ITEMS) if BATCH_OF[i] == BATCH_OF[n])


def part(start, n):
    return slice(start, start + n) if isinstance(start, int) else ds(start, n)


def squares_before(m):
    return D_TILES * m + (MID_SQUARES if m > RET_PHASE else 0)


def norms_before(m):
    return m + (RET_HEADS if m > RET_PHASE else 0)


def sums_before(m):
    return (D_TILES - 1) * m + ((RET_E_TILES - 1) * RET_HEADS if m > RET_PHASE else 0)


def width(ib):
    return (ib + 1) * P


def build(nc, t):
    ctx = ExitStack()

    def sb(name, shape, dt=F32):
        return ctx.enter_context(nc.sbuf_tensor(name, shape, dt))

    def sem(name):
        return ctx.enter_context(nc.semaphore(name))

    with ctx:
        staged = [sb(f"staged{s}", [P, UNIT]) for s in range(3)]
        w_hi_all = sb("w_hi", [P, 3, UNIT], F32R)
        w_lo_all = sb("w_lo", [P, 3, UNIT], F32R)
        w_hi = [w_hi_all[:, s, :] for s in range(3)]
        w_lo = [w_lo_all[:, s, :] for s in range(3)]
        h = sb("h", [P, D_TILES, SEQ])
        u_hi = sb("u_hi", [P, D_TILES, SEQ], F32R)
        u_lo = sb("u_lo", [P, D_TILES, SEQ], F32R)
        sq = sb("sq", [P, 2, SEQ])
        sq_sum = sb("sq_sum", [P, SEQ])
        rstd_b = sb("rstd_b", [P, SEQ])
        rstd_gb = sb("rstd_gb", [P, SEQ])
        std = sb("std", [P, TOK_TILES])
        rstd = sb("rstd", [P, TOK_TILES])
        std_g = sb("std_g", [P, TOK_TILES])
        rstd_g = sb("rstd_g", [P, TOK_TILES])
        eps = sb("eps", [P, 1])
        ones = sb("ones", [P, 1])
        ident = sb("ident", [P, P])
        ident_bf = sb("ident_bf", [P, P], BF16)
        causal_neg = sb("causal_neg", [P, P])
        causal_neg_bf = sb("causal_neg_bf", [P, P], BF16)
        cmp_mask = sb("cmp_mask", [P, TOK_TILES, CMP_PAD])
        cmp_neg = sb("cmp_neg", [P, TOK_TILES, CMP_PAD])
        rows = sb("rows", [N_ROWS, P])
        cols = sb("cols", [P, N_ROWS])
        work = sb("work", [P, WORK])
        parts = sb("parts", [P, PARTS], F32R)

        taken = {}

        def area(phase, size, *shape, of=work):
            key = phase, of is work
            at = taken.get(key, 0)
            taken[key] = at + size
            assert at + size <= (WORK if of is work else PARTS), phase
            v = of[:, at:at + size]
            if len(shape) == 2:
                v = v.rearrange("p (a b) -> p a b", a=shape[0])
            elif len(shape) == 3:
                v = v.rearrange("p (a b c) -> p a b c", a=shape[0], b=shape[1])
            return v

        x_tok = area("start", TOK_TILES * D_MODEL, TOK_TILES, D_MODEL)
        mid_hi = area("ret", 4 * SEQ, 4, SEQ, of=parts)
        mid_lo = area("ret", 4 * SEQ, 4, SEQ, of=parts)
        a_scaled_t = area("ffn", 2 * SEQ, 2, SEQ)
        silu_a = area("ffn", 2 * SEQ, 2, SEQ)
        silu_r = area("ffn", 2 * SEQ, 2, SEQ)
        hid = area("ffn", 2 * SEQ, 2, SEQ)
        taken["ret", False] = 0
        area("ret", 8 * SEQ, of=parts)
        r_hi = [area("ret", 2 * SEQ, 2, SEQ, of=parts) for _ in range(2)]
        r_lo = [area("ret", 2 * SEQ, 2, SEQ, of=parts) for _ in range(2)]
        r_v = area("ret", TOK_TILES * SEQ, TOK_TILES, SEQ)
        r_g = area("ret", RET_E_TILES * SEQ, RET_E_TILES, SEQ)
        cos_t = area("ret", SEQ)
        sin_t = area("ret", SEQ)
        decay = area("ret", RET_HEADS * SEQ)
        r_out = area("ret", 2 * SEQ, 2, SEQ)
        r_p = area("ret", sum(SEQ - jb * P for jb in range(TOK_TILES)))
        r_p_at = [sum(SEQ - j * P for j in range(jb)) for jb in range(TOK_TILES)]
        taken["end", True] = TOK_TILES * D_MODEL
        y = area("end", D_TILES * SEQ, D_TILES, SEQ)
        c_x = area("cmp", CMP_K_TILES * N_WIN, CMP_K_TILES, N_WIN)
        c_t = area("cmp", NSA_GROUPS * SEQ, NSA_GROUPS, SEQ)
        area("cmp", 8 * SEQ, of=parts)
        c_hid_tok = area("cmp", CMP_HID)
        c_hid = area("cmp", 2 * N_WIN, 2, N_WIN)
        gates_fm = area("cmp", SEQ)
        c_xhi = area("cmp", CMP_K_TILES * N_WIN, CMP_K_TILES, N_WIN, of=parts)
        c_xlo = area("cmp", CMP_K_TILES * N_WIN, CMP_K_TILES, N_WIN, of=parts)
        v_all = work[:, WORK - V_WORDS:].rearrange("p (a b c) -> p a b c", a=TOK_TILES, b=2)
        assert taken["cmp", True] <= WORK - V_WORDS
        n_p = area("nsa", 3 * 2 * SEQ, 3, 2, SEQ)
        n_pt = area("nsa", 2 * 2 * SEQ, 2, 2, SEQ)
        n_v = area("nsa", TOK_TILES * 2 * NSA_DH, TOK_TILES, 2, NSA_DH)
        n_f32 = n_p[:, 0:2, 0, :]
        n_kf32 = n_p[:, 2, 0, :]
        c_s = area("nsa", 16 * CMP_PAD, 16, CMP_PAD)
        c_p = area("nsa", 16 * CMP_PAD, 16, CMP_PAD)
        c_pt = rstd_gb[:].rearrange("p (a q) -> p a q", a=4)
        c_vg = area("nsa", TOK_TILES * NSA_DH, TOK_TILES, NSA_DH)
        gate_g = area("nsa", 3 * 16, 3, 16)
        c_max = area("nsa", 16)
        c_den = area("nsa", 16)
        c_rden = area("nsa", 16)
        c_fac = area("nsa", 16)
        s_max = area("nsa", 8)
        s_bias = area("nsa", 8)
        s_den = area("nsa", 8)
        s_rden = area("nsa", 8)
        assert taken["nsa", True] <= WORK - V_WORDS
        n_qhi = mid_hi[:, 2:4, :]
        n_qlo = mid_lo[:, 2:4, :]
        area("nsa", 8 * SEQ, of=parts)
        n_khi = area("nsa", 4 * SEQ, 2, 2, SEQ, of=parts)
        n_klo = area("nsa", 4 * SEQ, 2, 2, SEQ, of=parts)
        c_kghi = area("nsa", 2 * CMP_PAD, 2, CMP_PAD, of=parts)
        c_kglo = area("nsa", 2 * CMP_PAD, 2, CMP_PAD, of=parts)
        c_w2 = sb("c_w2", [P, 2, 2, 2 * NSA_DH])
        c_khi = sb("c_khi", [P, NSA_GROUPS, CMP_PAD], F32R)
        c_klo = sb("c_klo", [P, NSA_GROUPS, CMP_PAD], F32R)
        c_v = sb("c_v", [CMP_PAD, NSA_GROUPS, NSA_DH])
        gates = sb("gates", [P, TOK_TILES, N_GATES])

        banks2 = [ctx.enter_context(nc.psum_tensor(f"banks{b}", [P, 2, SEQ], F32)) for b in range(4)]
        bank = [banks2[b // 2][:, b % 2, :] for b in range(8)]

        loaded = [sem(f"loaded{s}") for s in range(3)]
        split_hi = [sem(f"split_hi{s}") for s in range(3)]
        split_lo = [sem(f"split_lo{s}") for s in range(3)]
        unit_used = [sem(f"unit_used{s}") for s in range(3)]
        rows_loaded = sem("rows_loaded")
        const_loaded = sem("const_loaded")
        x_loaded = [sem(f"x_loaded{a}") for a in range(TOK_TILES)]
        const_set = sem("const_set")
        const_derived = sem("const_derived")
        rows_turned = sem("rows_turned")
        cols_ready = sem("cols_ready")
        x_turned = sem("x_turned")
        y_ready = sem("y_ready")
        y_turned = sem("y_turned")
        y_copied = [sem(f"y_copied{i}") for i in range(2)]
        stored = sem("stored")
        out_ready = sem("out_ready")
        h_added = sem("h_added")
        squared = sem("squared")
        sq_summed = sem("sq_summed")
        sumsq_ready = sem("sumsq_ready")
        std_ready = sem("std_ready")
        rstd_ready = sem("rstd_ready")
        rstd_spread = sem("rstd_spread")
        rstd_copied = sem("rstd_copied")
        u_hi_ready = sem("u_hi_ready")
        u_ready = sem("u_ready")
        a_ready = sem("a_ready")
        b_ready = sem("b_ready")
        a_scaled = sem("a_scaled")
        silu_r_ready = sem("silu_r_ready")
        silu_ready = sem("silu_ready")
        hid_ready = sem("hid_ready")
        mid_hi_ready = sem("mid_hi_ready")
        mid_ready = sem("mid_ready")
        ret_loaded = sem("ret_loaded")
        qk_ready = sem("qk_ready")
        rot_products = sem("rot_products")
        tables_scaled = sem("tables_scaled")
        rotated = sem("rotated")
        rot_hi = sem("rot_hi")
        rot_ready = sem("rot_ready")
        v_ready = sem("v_ready")
        v_copied = sem("v_copied")
        scores_ready = sem("scores_ready")
        decayed = sem("decayed")
        g_ready = sem("g_ready")
        g_scaled = sem("g_scaled")
        silu_g_ready = sem("silu_g_ready")
        o_ready = sem("o_ready")
        gated = sem("gated")
        out_scaled = sem("out_scaled")
        z_hi_ready = sem("z_hi_ready")
        z_ready = sem("z_ready")
        ct_ready = sem("ct_ready")
        ct_copied = sem("ct_copied")
        gates_copied = sem("gates_copied")
        gates_turned = sem("gates_turned")
        cx_added = sem("cx_added")
        cx_hi = sem("cx_hi")
        cx_split = sem("cx_split")
        chid_silu = sem("chid_silu")
        chid_turned = sem("chid_turned")
        chid_copied = sem("chid_copied")
        ckv_ready = sem("ckv_ready")
        ckv_copied = sem("ckv_copied")
        ck_hi = sem("ck_hi")
        gates_set = sem("gates_set")
        gq_ready = sem("gq_ready")
        gq_scaled = sem("gq_scaled")
        gq_hi = sem("gq_hi")
        gq_split = sem("gq_split")
        gk_scaled = sem("gk_scaled")
        gk_hi = sem("gk_hi")
        gk_split = sem("gk_split")
        v_all_ready = sem("v_all_ready")
        v_all_set = sem("v_all_set")
        group_set = sem("group_set")
        halves_zeroed = sem("halves_zeroed")
        cs_ready = sem("cs_ready")
        cs_steps = sem("cs_steps")
        cs_exp = sem("cs_exp")
        cpt_ready = sem("cpt_ready")
        cpt_copied = sem("cpt_copied")
        s_ready = sem("s_ready")
        s_maxed = sem("s_maxed")
        s_biased = sem("s_biased")
        s_exp = sem("s_exp")
        s_recip = sem("s_recip")
        p_ready = sem("p_ready")
        pt_ready = sem("pt_ready")
        pt_copied = [sem(f"pt_copied{i}") for i in range(2)]
        pv_done = sem("pv_done")
        no_hi_ready = sem("no_hi_ready")
        no_split = sem("no_split")

        def in_view(s):
            return s.rearrange("p (k c) -> p k c", k=D_TILES)

        def key_view(s):
            return s[:, 0:D_TILES * P].rearrange("p (k c) -> p k c", k=D_TILES)

        def v_view(s):
            return s.rearrange("p (k c) -> p k c", k=4)

        def out_view(s):
            return s.rearrange("p (k c) -> p k c", k=2)

        def tiled(w):
            return w.rearrange("(k p) c -> p k c", p=P)

        ffn_w_in = {0: tiled(t["ffn1_w_in"][0]), 2: tiled(t["ffn2_w_in"][0]),
                    3: tiled(t["ffn1_w_in"][1]), 5: tiled(t["ffn2_w_in"][1])}
        ffn_w_out = {0: tiled(t["ffn1_w_out"][0]), 2: tiled(t["ffn2_w_out"][0]),
                     3: tiled(t["ffn1_w_out"][1]), 5: tiled(t["ffn2_w_out"][1])}
        ret_w_in = tiled(t["ret_w_in"][0])
        ret_w_out = tiled(t["ret_w_out"][0])
        nsa_w_in = tiled(t["nsa_w_in"][0])
        nsa_w_out = tiled(t["nsa_w_out"][0])

        block = ctx.enter_context(nc.Block())

        @block.sync
        def _(sp):
            def load(slot, use, pieces):
                if not isinstance(use, int) or use > 0:
                    sp.wait_ge(split_lo[slot], use)
                for dst, src in pieces:
                    sp.dma_start(dst, src).then_inc(loaded[slot], 16)

            def load_ffn(ph, j, pieces=1):
                s, n = USES0[ph], D_TILES // pieces
                load(0, s[0] + j, [(in_view(staged[0][:]), ffn_w_in[ph][:, :, ds(j * PAIR, PAIR)])])
                load(1, s[1] + j, [(in_view(staged[1][:])[:, k:k + n, :],
                                    ffn_w_in[ph][:, k:k + n, ds(j * PAIR + D_FF, PAIR)])
                                   for k in range(0, D_TILES, n)])
                load(2, s[2] + j, [(out_view(staged[2][:]), ffn_w_out[ph][:, ds(j * 2, 2), :])])

            def load_ret(hd):
                s = USES0[RET_PHASE]
                load(0, s[0] + hd * 3, [(in_view(staged[0][:]), ret_w_in[:, :, ds(hd * RET_DK, PAIR)])])
                load(1, s[1] + hd * 3, [(in_view(staged[1][:]), ret_w_in[:, :, ds(hd * RET_DK + RET_K0, PAIR)])])
                load(2, s[2] + hd * 2, [(v_view(staged[2][:]), ret_w_in[:, 0:4, ds(hd * RET_DV + RET_V0, RET_DV)])])
                load(0, s[0] + hd * 3 + 1, [(v_view(staged[0][:]), ret_w_in[:, 4:8, ds(hd * RET_DV + RET_V0, RET_DV)])])
                load(1, s[1] + hd * 3 + 1, [(in_view(staged[1][:]), ret_w_in[:, :, ds(hd * RET_DV + RET_G0, PAIR)])])
                load(2, s[2] + hd * 2 + 1,
                     [(in_view(staged[2][:]), ret_w_in[:, :, ds(hd * RET_DV + (RET_G0 + PAIR), PAIR)])])
                load(0, s[0] + hd * 3 + 2, [(out_view(staged[0][:]), ret_w_out[:, ds(hd * 4, 2), :])])
                load(1, s[1] + hd * 3 + 2, [(out_view(staged[1][:]), ret_w_out[:, ds(hd * 4 + 2, 2), :])])

            def load_nsa(g, s):
                load(1, s[1] + g, [(key_view(staged[1])[:, :, i * NSA_DH:(i + 1) * NSA_DH],
                                    nsa_w_in[:, :, ds(g * NSA_DH + (NSA_KV0 + c * NSA_HKV), NSA_DH)])
                                   for i, c in enumerate((2, 4))])
                load(0, s[0] + g, [(in_view(staged[0][:]), nsa_w_in[:, :, ds(g * PAIR, PAIR)])])
                load(2, s[2] + g, [(out_view(staged[2][:]), nsa_w_out[:, ds(g * 2, 2), :])])

            sp.dma_start(ident[:], t["c_ident"]).then_inc(rows_loaded, 16)
            src = t["x"][0].rearrange("(a p) d -> p a d", p=P)
            for a in range(TOK_TILES):
                sp.dma_start(x_tok[:, a, :], src[:, a, :]).then_inc(x_loaded[a], 16)
            at = 0
            for name in ("norm_ffn1", "norm_mix", "norm_ffn2"):
                sp.dma_start(rows[at:at + 16, :], t[name].rearrange("l (d p) -> (l d) p", p=P)).then_inc(rows_loaded, 16)
                at += 16
            sp.dma_start(rows[at:at + 8, :], t["norm_final"].rearrange("(d p) -> d p", p=P)).then_inc(rows_loaded, 16)
            sp.dma_start(rows[ROW_GN:ROW_GN + 16, :], t["ret_gn_gain"][0].rearrange("(d p) -> d p", p=P))\
              .then_inc(rows_loaded, 16)
            sp.dma_start(rows[ROW_POS:N_ROWS, :],
                         t["nsa_cmp_pos"][0].rearrange("c (k l) d -> (c k) (l d)", l=2)).then_inc(rows_loaded, 16)
            load(0, 0, [(in_view(staged[0][:]), ffn_w_in[0][:, :, 0:PAIR])])
            load(1, 0, [(in_view(staged[1][:]), ffn_w_in[0][:, :, D_FF:D_FF + PAIR])])
            load(2, 0, [(out_view(staged[2][:]), ffn_w_out[0][:, 0:2, :])])
            sp.dma_start(causal_neg[:], t["c_causal"]).then_inc(const_loaded, 16)
            sp.dma_start(cmp_mask[:], t["c_cmp_mask"]).then_inc(const_loaded, 16)
            for c in range(2):
                for i in range(2):
                    sp.dma_start(c_w2[:, c, :, i * NSA_DH:(i + 1) * NSA_DH],
                                 tiled(t["nsa_cmp_w2"][0, c])).then_inc(const_loaded, 16)

            with sp.Fori(1, FF_PAIRS) as j:
                load_ffn(0, j)
            sp.dma_start(cos_t, t["c_cos"]).then_inc(ret_loaded, 16)
            sp.dma_start(sin_t, t["c_sin"]).then_inc(ret_loaded, 16)
            sp.dma_start(decay, t["c_decay"]).then_inc(ret_loaded, 16)
            with sp.Fori(0, RET_HEADS) as hd:
                load_ret(hd)
            with sp.Fori(0, FF_PAIRS) as j:
                load_ffn(2, j)
            with sp.Fori(0, FF_PAIRS) as j:
                load_ffn(3, j)
            s = USES0[NSA_PHASE]
            for c in range(2):
                load(c, s[c], [(in_view(staged[c][:]),
                                nsa_w_in[:, :, NSA_KV0 + c * NSA_HKV:NSA_KV0 + (c + 1) * NSA_HKV])])
            load(2, s[2], [(staged[2][:, 0:D_TILES * N_GATES].rearrange("p (k c) -> p k c", k=D_TILES),
                            nsa_w_in[:, :, NSA_GATE0:NSA_GATE0 + N_GATES])])
            for n, slot in enumerate((0, 2)):
                col = NSA_KV0 + (3 + 2 * n) * NSA_HKV
                load(slot, s[slot] + 1, [(in_view(staged[slot][:]), nsa_w_in[:, :, col:col + NSA_HKV])])
            for slot, use, c, half in ((1, 1, 0, 0), (2, 2, 1, 0), (0, 2, 1, 1), (1, 2, 0, 1)):
                load(slot, s[slot] + use, [(in_view(staged[slot][:]),
                                            tiled(t["nsa_cmp_w1"][0, c])[:, D_TILES * half:D_TILES * (half + 1), :])])
            with sp.Fori(0, NSA_GROUPS) as g:
                load_nsa(g, [n + first for n, first in zip(s, NSA_FIRST)])
            load_ffn(5, 0, KEY_PIECES)
            with sp.Fori(1, FF_PAIRS) as j:
                load_ffn(5, j)
            for n in range(2 * TOK_TILES):
                half, a = n // TOK_TILES, n % TOK_TILES
                sp.wait_ge(y_copied[a % 2], 2 * half + a // 2 + 1)
                sp.dma_start(t["out"][0, a * P:(a + 1) * P, half * SEQ:(half + 1) * SEQ],
                             x_tok[:, a, half * SEQ:(half + 1) * SEQ]).then_inc(stored, 16)
            sp.wait_ge(stored, 16 * 2 * TOK_TILES)

        def loaded_value(slot, use, group=None):
            if slot == 1 and group is not None:
                return (USES0[NSA_PHASE][1] + NSA_FIRST[1]) * 16 + (group + 1) * (16 * KEY_PIECES)
            return use * 16 + 16

        def item_scores(n):
            pair, ib, par = ITEMS[n]
            at = par * width(ib) if len(BATCHES[BATCH_OF[n]][2]) == 2 else 0
            return banks2[BATCH_OF[n] % 2][:, :, at:at + width(ib)]

        @block.tensor
        def _(pe):
            def products(out, l_hi, l_lo, r_hi, r_lo, first, last):
                pe.matmul(out, l_hi, r_hi, start=first, stop=False)
                pe.matmul(out, l_hi, r_lo, start=False, stop=False)
                return pe.matmul(out, l_lo, r_hi, start=False, stop=last)

            def project_pair(slot, banks, ready, need_u=None, between=None):
                hi, lo = in_view(w_hi[slot]), in_view(w_lo[slot])
                for i, b in enumerate(banks):
                    for k in range(D_TILES):
                        if need_u is not None and i == 0:
                            pe.wait_ge(u_ready, need_u + k + 1)
                        m = products(b, hi[:, k, i * P:(i + 1) * P], lo[:, k, i * P:(i + 1) * P],
                                     u_hi[:, k, :], u_lo[:, k, :], k == 0, k == D_TILES - 1)
                    if i == 0:
                        m.then_inc(ready, 1)
                        if between is not None:
                            between()
                m.then_inc(unit_used[slot], 1)

            def sum_squares(sums, out):
                pe.wait_ge(sq_summed, sums)
                for a in range(TOK_TILES):
                    m = pe.matmul(out[:, a:a + 1], sq_sum[:, a * P:(a + 1) * P], ones[:, 0:1], start=True, stop=True)
                m.then_inc(sumsq_ready, 1)

            def spread(q, src, out):
                pe.wait_ge(rstd_ready, q + 1)
                for a in range(TOK_TILES):
                    m = pe.matmul(out[:, a * P:(a + 1) * P], src[:, a:a + 1].to_broadcast([P, P]), ident[:],
                                  start=True, stop=True)
                m.then_inc(rstd_spread, 1)

            def norm_sums(m):
                sum_squares(sums_before(m) + D_TILES - 1, bank[4])

            def norm_spread(m):
                spread(norms_before(m), rstd, bank[5])

            def ffn_a(ph, j, need_u=None):
                pe.wait_ge(split_lo[0], USES0[ph][0] + j + 1)
                if need_u is None:
                    pe.wait_ge(a_scaled, 2 * FF_PAIRS * FFN_NO[ph] + j * 2)
                project_pair(0, bank[0:2], a_ready, need_u)

            def ffn_b(ph, j, between=None):
                pe.wait_ge(split_lo[1], USES0[ph][1] + j + 1)
                if between is None:
                    pe.wait_ge(hid_ready, 2 * FF_PAIRS * FFN_NO[ph] + j * 2)
                project_pair(1, bank[2:4], b_ready, between=between)

            def out_tiles(tiles, ks):
                hi, lo = out_view(w_hi[2]), out_view(w_lo[2])
                for d, b in tiles:
                    for k in ks:
                        m = products(bank[b], hi[:, k, d * P:(d + 1) * P], lo[:, k, d * P:(d + 1) * P],
                                     mid_hi[:, k, :], mid_lo[:, k, :], k == 0, k == 1)
                    if ks[-1] == 1:
                        m.then_inc(out_ready if d < D_TILES - 1 else unit_used[2], 1)

            def ffn_out(ph, i, last=False):
                f = 2 * FF_PAIRS * FFN_NO[ph]
                before = OUT0[ph] + D_TILES + i * D_TILES
                pe.wait_ge(split_lo[2], USES0[ph][2] + i + 1)
                pe.wait_ge(h_added, before)
                if last:
                    pe.wait_ge(mid_ready, f + i * 2 + 1)
                    out_tiles([(d, 4 + d) for d in range(4)], (0,))
                    pe.wait_ge(mid_ready, f + i * 2 + 2)
                    out_tiles([(d, 4 + d) for d in range(4)], (1,))
                else:
                    pe.wait_ge(mid_ready, f + i * 2 + 2)
                    out_tiles([(d, 4 + d) for d in range(4)], (0, 1))
                for d in range(4, D_TILES):
                    pe.wait_ge(h_added, before + (d - 3))
                    out_tiles([(d, d)], (0, 1))

            def ffn(ph):
                ffn_a(ph, 0, need_u=D_TILES * ph)
                norm_sums(ph)
                ffn_b(ph, 0, between=lambda: norm_spread(ph))
                with pe.Fori(1, FF_PAIRS) as j:
                    ffn_a(ph, j)
                    ffn_out(ph, j - 1)
                    ffn_b(ph, j)
                ffn_out(ph, FF_PAIRS - 1, last=True)

            def retention_head(hd, first=False):
                s = USES0[RET_PHASE]
                pe.wait_ge(split_lo[0], s[0] + hd * 3 + 1)
                if not first:
                    pe.wait_ge(out_scaled, hd * 8 - 2)
                project_pair(0, bank[0:2], qk_ready, need_u=D_TILES * RET_PHASE if first else None)
                pe.wait_ge(split_lo[1], s[1] + hd * 3 + 1)
                if first:
                    norm_sums(RET_PHASE)
                else:
                    pe.wait_ge(out_scaled, hd * 8)
                project_pair(1, bank[2:4], qk_ready, between=(lambda: norm_spread(RET_PHASE)) if first else None)
                if first:
                    pe.wait_ge(rstd_copied, RET_PHASE + 1)
                for n, slot, use in ((0, 2, s[2] + hd * 2), (1, 0, s[0] + hd * 3 + 1)):
                    hi, lo = v_view(w_hi[slot]), v_view(w_lo[slot])
                    pe.wait_ge(split_lo[slot], use + 1)
                    for a in range(TOK_TILES):
                        for k in range(4):
                            d = 4 * n + k
                            m = products(bank[4 + a], u_hi[:, d, a * P:(a + 1) * P], u_lo[:, d, a * P:(a + 1) * P],
                                         hi[:, k, :], lo[:, k, :], d == 0, d == D_TILES - 1)
                        if n == 1 and a < TOK_TILES - 1:
                            m.then_inc(v_ready, 1)
                    m.then_inc(unit_used[slot], 1)
                pe.wait_ge(rot_ready, hd * 4 + 4)
                for jb in range(TOK_TILES):
                    keys, queries = slice(jb * P, (jb + 1) * P), slice(jb * P, SEQ)
                    for c in range(2):
                        m = products(bank[jb][:, 0:SEQ - jb * P], r_hi[1][:, c, keys], r_lo[1][:, c, keys],
                                     r_hi[0][:, c, queries], r_lo[0][:, c, queries], c == 0, c == 1)
                    m.then_inc(scores_ready, 1)
                for n, slot, use in ((0, 1, s[1] + hd * 3 + 1), (1, 2, s[2] + hd * 2 + 1)):
                    pe.wait_ge(split_lo[slot], use + 1)
                    pe.wait_ge(v_copied, hd * 4 + 2 * n + 2)
                    project_pair(slot, bank[4 + 2 * n:6 + 2 * n], g_ready)
                pe.wait_ge(v_copied, hd * 4 + 4)
                pe.wait_ge(decayed, hd * 4 + 4)
                for e in range(RET_E_TILES):
                    for jb in range(TOK_TILES):
                        m = pe.matmul(bank[e][:, jb * P:SEQ], r_v[:, jb, e * P:(e + 1) * P],
                                      r_p[:, r_p_at[jb]:r_p_at[jb] + SEQ - jb * P],
                                      start=jb == 0, stop=jb == TOK_TILES - 1)
                    m.then_inc(o_ready, 1)
                def out(n, tiles):
                    hi, lo = out_view(w_hi[n]), out_view(w_lo[n])
                    for d in tiles:
                        for k in range(2):
                            m = products(bank[RET_OUT_BANK[d]], hi[:, k, d * P:(d + 1) * P], lo[:, k, d * P:(d + 1) * P],
                                         mid_hi[:, 2 * n + k, :], mid_lo[:, 2 * n + k, :],
                                         n == 0 and k == 0, n == 1 and k == 1)
                        if d == D_TILES - 1:
                            m.then_inc(unit_used[n], 1)
                        elif n == 1:
                            m.then_inc(out_ready, 1)

                pe.wait_ge(split_lo[0], s[0] + hd * 3 + 3)
                pe.wait_ge(g_scaled, hd * 4 + 4)
                pe.wait_ge(z_ready, hd * 4 + 2)
                out(0, range(0, 4))
                pe.wait_ge(z_ready, hd * 4 + 4)
                out(0, range(4, 7))
                sum_squares((D_TILES - 1) * 2 + (hd + 1) * (RET_E_TILES - 1), bank[3])
                pe.wait_ge(split_lo[1], s[1] + hd * 3 + 3)
                out(1, range(0, 1))
                spread(hd + 2, rstd_g, bank[3])
                out(1, range(1, 2))
                pe.wait_ge(rstd_copied, hd + 3)
                out(0, range(7, 8))
                out(1, range(2, 8))

            def compression():
                s = USES0[NSA_PHASE]
                pe.wait_ge(split_lo[0], s[0] + 1)
                project_pair(0, bank[0:2], ct_ready, need_u=D_TILES * NSA_PHASE)
                norm_sums(NSA_PHASE)
                hi = w_hi[2][:, 0:D_TILES * N_GATES].rearrange("p (k c) -> p k c", k=D_TILES)
                lo = w_lo[2][:, 0:D_TILES * N_GATES].rearrange("p (k c) -> p k c", k=D_TILES)
                pe.wait_ge(split_lo[2], s[2] + 1)
                for k in range(D_TILES):
                    m = products(bank[7][0:N_GATES, :], hi[:, k, :], lo[:, k, :], u_hi[:, k, :], u_lo[:, k, :],
                                 k == 0, k == D_TILES - 1)
                m.then_inc(unit_used[2], 1)

                def after_first():
                    norm_spread(NSA_PHASE)
                    pe.wait_ge(gates_copied, 1)
                    for a in range(TOK_TILES):
                        m = pe.transpose(bank[7][:, a * N_GATES:(a + 1) * N_GATES],
                                         gates_fm[0:N_GATES, a * P:(a + 1) * P], ident[0:N_GATES, 0:N_GATES])
                    m.then_inc(gates_turned, 1)

                pe.wait_ge(split_lo[1], s[1] + 1)
                project_pair(1, bank[2:4], ct_ready, between=after_first)
                hi_2, lo_2 = ([v[:, 0:3:2, k * PAIR:(k + 1) * PAIR] for k in range(D_TILES)] for v in (w_hi_all, w_lo_all))

                def all_values(a):
                    if a == 0:
                        pe.wait_ge(split_lo[0], s[0] + 2)
                        pe.wait_ge(split_lo[2], s[2] + 2)
                    if a % 2 == 0:
                        pe.wait_ge(ct_copied, 8 * (a // 2 + 1))
                    out = bank[a].rearrange("p (b c) -> p b c", b=2)
                    tokens = slice(a * P, (a + 1) * P)
                    for k in range(D_TILES - 1):
                        products(out, u_hi[:, k, tokens], u_lo[:, k, tokens], hi_2[k], lo_2[k], k == 0, False)
                    k = D_TILES - 1
                    pe.matmul(out, u_hi[:, k, tokens], hi_2[k], start=False, stop=False)
                    pe.matmul(out, u_hi[:, k, tokens], lo_2[k], start=False, stop=False)
                    if a < TOK_TILES - 1:
                        pe.matmul(out, u_lo[:, k, tokens], hi_2[k], start=False, stop=True).then_inc(v_all_ready, 1)
                    else:
                        for b, slot in ((1, 2), (0, 0)):
                            pe.matmul(out[:, b, :], u_lo[:, k, tokens], hi_2[k][:, b, :], start=False, stop=b == 0)\
                              .then_inc(unit_used[slot], 1)

                def hidden(c, half, slot, use):
                    hi, lo = in_view(w_hi[slot]), in_view(w_lo[slot])
                    pe.wait_ge(cx_split, 2 * c + half + 1)
                    pe.wait_ge(split_lo[slot], s[slot] + use + 1)
                    for k in range(D_TILES):
                        kk = half * D_TILES + k
                        m = products(bank[4 + c][0:N_WIN, 0:CMP_HID], c_xhi[:, kk, :], c_xlo[:, kk, :], hi[:, k, :],
                                     lo[:, k, :], kk == 0, kk == CMP_K_TILES - 1)
                    m.then_inc(unit_used[slot], 1)

                def turn_hidden(c):
                    pe.wait_ge(chid_silu, c + 1)
                    if c == 1:
                        pe.wait_ge(chid_copied, 1)
                    for m2 in range(2):
                        m = pe.transpose(bank[6][:, m2 * N_WIN:(m2 + 1) * N_WIN],
                                         c_hid_tok[0:N_WIN, m2 * P:(m2 + 1) * P], ident[0:N_WIN, 0:N_WIN])
                    m.then_inc(chid_turned, 1)

                all_values(0)
                all_values(1)
                pe.wait_ge(rstd_copied, norms_before(NSA_PHASE) + 1)
                hidden(0, 0, 1, 1)
                all_values(2)
                hidden(0, 1, 1, 2)
                all_values(3)
                turn_hidden(0)
                pe.wait_ge(gates_set, 4)
                pe.wait_ge(chid_copied, 1)
                for m2 in range(2):
                    m = pe.matmul(bank[7][:, 0:N_WIN], c_w2[:, 0, m2, :], c_hid[:, m2, :], start=m2 == 0, stop=m2 == 1)
                m.then_inc(ckv_ready, 1)
                hidden(1, 0, 2, 2)
                hidden(1, 1, 0, 2)
                turn_hidden(1)
                pe.wait_ge(ckv_copied, 1)
                pe.wait_ge(chid_copied, 2)
                for g in range(NSA_GROUPS):
                    for m2 in range(2):
                        m = pe.matmul(bank[7][0:N_CMP, g * NSA_DH:(g + 1) * NSA_DH],
                                      c_hid[:, m2, g * N_CMP:(g + 1) * N_CMP], c_w2[:, 1, m2, 0:NSA_DH],
                                      start=m2 == 0, stop=m2 == 1)
                m.then_inc(ckv_ready, 1)

            def nsa_group(g):
                s = USES0[NSA_PHASE]
                before = OUT0[NSA_PHASE] + D_TILES + g * D_TILES
                hi, lo = key_view(w_hi[1]), key_view(w_lo[1])
                pe.wait_ge(split_lo[1], s[1] + g + (NSA_FIRST[1] + 1))
                pe.wait_ge(v_all_set, TOK_TILES)
                pe.wait_ge(h_added, before - 3)
                for k in range(D_TILES):
                    m = products(bank[0], hi[:, k, :], lo[:, k, :], u_hi[:, k, :], u_lo[:, k, :],
                                 k == 0, k == D_TILES - 1)
                m.then_inc(unit_used[1], 1)
                pe.wait_ge(split_lo[0], s[0] + g + (NSA_FIRST[0] + 1))
                pe.wait_ge(h_added, before)
                project_pair(0, bank[2:4], gq_ready)
                pe.wait_ge(halves_zeroed, 5)
                pe.wait_ge(const_derived, 3)
                pe.wait_ge(group_set, g * GROUP_SETS + GROUP_SETS)

                def compressed_scores(pair):
                    pe.wait_ge(gq_split, g * 2 + (pair + 1))
                    for ib in range(TOK_TILES):
                        at = (pair * TOK_TILES + ib) * 2 * CMP_PAD
                        m = products(bank[4][:, at:at + 2 * CMP_PAD].rearrange("p (a n) -> p a n", a=2),
                                     n_qhi[:, pair, ib * P:(ib + 1) * P], n_qlo[:, pair, ib * P:(ib + 1) * P],
                                     c_kghi, c_kglo, True, True)
                    if pair == 1:
                        m.then_inc(cs_ready, 1)

                def scores(b):
                    pair, ib, pars = BATCHES[b]
                    if b == 0:
                        pe.wait_ge(gk_split, g * 4 + 4)
                    elif b > 1:
                        last = batch_end(BATCH_OF.index(b - 2))
                        pe.wait_ge(s_exp, g * (2 * N_ITEMS) + 2 * (last + 1))
                    queries, w = slice(ib * P, (ib + 1) * P), width(ib)
                    heads = slice(pars[0], pars[-1] + 1)
                    for br in range(2):
                        out = banks2[b % 2][:, br, :]
                        products(out[:, 0:len(pars) * w].rearrange("p (a n) -> p a n", a=len(pars)),
                                 n_qhi[:, pair, queries], n_qlo[:, pair, queries],
                                 n_khi[:, br, heads, 0:w], n_klo[:, br, heads, 0:w], True, False)
                        for i in range(len(pars)):
                            pe.matmul(out[:, i * w + ib * P:(i + 1) * w], ident_bf[:], causal_neg_bf[:],
                                      start=False, stop=i == len(pars) - 1).then_inc(s_ready, 1)

                def turn(n):
                    pair, ib, par = ITEMS[n]
                    for br in range(2):
                        pe.wait_ge(p_ready, g * (2 * N_ITEMS) + (2 * n + br + 1))
                        if n >= 1:
                            pe.wait_ge(pt_copied[br], g * N_ITEMS + n)
                        for jb in range(ib + 1):
                            m = pe.transpose(bank[4 + br][:, jb * P:(jb + 1) * P],
                                             n_p[:, n % 3, br, jb * P:(jb + 1) * P], ident[:])
                        m.then_inc(pt_ready, 1)

                def values(n):
                    pair, ib, par = ITEMS[n]
                    o = bank[6 + pair][par * NSA_DH:(par + 1) * NSA_DH, ib * P:(ib + 1) * P]
                    for br in range(2):
                        pe.wait_ge(pt_copied[br], g * N_ITEMS + (n + 1))
                        for jb in range(ib + 1):
                            m = pe.matmul(o, n_v[:, jb, br, :], n_pt[:, n % 2, br, jb * P:(jb + 1) * P],
                                          start=False, stop=False)
                    if n >= LATE_ITEMS:
                        m = compressed_values(n)
                    m.then_inc(pv_done, 1)

                def compressed_values(n):
                    pair, ib, par = ITEMS[n]
                    return pe.matmul(bank[6 + pair][par * NSA_DH:(par + 1) * NSA_DH, ib * P:(ib + 1) * P], c_vg[:, ib, :],
                                     c_pt[:, par * 2 + pair, :], start=False, stop=ib == TOK_TILES - 1)

                def clear(pair):
                    zeros = ident_bf[0:NSA_DH, P - 1:P].to_broadcast([NSA_DH, SEQ])
                    pe.matmul(bank[6 + pair], ident_bf[0:NSA_DH, :], zeros, start=True, stop=False)

                compressed_scores(0)
                scores(0)
                compressed_scores(1)
                scores(1)
                for n in range(N_ITEMS + 1):
                    if n < N_ITEMS and n == batch_end(n) and BATCH_OF[n] + 2 < len(BATCHES):
                        scores(BATCH_OF[n] + 2)
                    if n == LATE_ITEMS - 1:
                        pe.wait_ge(cs_steps, g * CS_STEPS + CS_STEPS)
                        for i in range(NSA_HPG):
                            m = pe.transpose(bank[7][:, i * P:(i + 1) * P],
                                             c_p[:, i * TOK_TILES:(i + 1) * TOK_TILES, :].rearrange("p i n -> p (i n)"),
                                             ident[:])
                        m.then_inc(cpt_ready, 1)
                    if n == 1:
                        clear(0)
                    if n == N_ITEMS // 2 + 1:
                        clear(1)
                    if n >= 1:
                        values(n - 1)
                    if n == LATE_ITEMS:
                        pe.wait_ge(cpt_copied, g + 1)
                        for late in range(LATE_ITEMS):
                            compressed_values(late)
                    if n < N_ITEMS:
                        turn(n)
                pe.wait_ge(split_lo[2], s[2] + g + (NSA_FIRST[2] + 1))
                pe.wait_ge(no_split, g * 2 + 1)
                out_tiles([(d, d) for d in range(4)], (0,))
                pe.wait_ge(no_split, g * 2 + 2)
                out_tiles([(d, d) for d in range(4)], (1,))
                for d in range(4, D_TILES):
                    pe.wait_ge(h_added, before + (d - 3))
                    out_tiles([(d, d - 4)], (0, 1))

            pe.wait_ge(const_set, 5)
            pe.wait_ge(rows_loaded, 16 * 7)
            pe.transpose(bank[7][:, 0:N_ROWS], rows[:], ident[0:N_ROWS, 0:N_ROWS]).then_inc(rows_turned, 1)
            for a in range(TOK_TILES):
                pe.wait_ge(x_loaded[a], 16)
                for d in range(D_TILES):
                    if a == 0 and d == D_TILES - 1:
                        pe.wait_ge(cols_ready, 1)
                    m = pe.transpose(bank[d][:, a * P:(a + 1) * P], x_tok[:, a, d * P:(d + 1) * P], ident[:])
                    if a == TOK_TILES - 1:
                        m.then_inc(x_turned, 1)
            ffn(0)
            retention_head(0, first=True)
            with pe.Fori(1, RET_HEADS - 1) as hd:
                retention_head(hd)
            retention_head(RET_HEADS - 1)
            pe.wait_ge(out_scaled, RET_HEADS * 8 - 2)
            ffn(2)
            ffn(3)
            compression()
            with pe.Fori(0, NSA_GROUPS) as g:
                nsa_group(g)
            ffn(5)
            for d in range(4):
                pe.wait_ge(y_ready, d + 1)
                for a in range(TOK_TILES):
                    m = pe.transpose(bank[a][:, d * P:(d + 1) * P], y[:, d, a * P:(a + 1) * P], ident[:])
                    if d == 3:
                        m.then_inc(y_turned, 1)
            pe.wait_ge(y_ready, D_TILES)
            for a in range(TOK_TILES):
                if a == TOK_TILES - 1:
                    sum_squares(sums_before(N_PHASES) + D_TILES - 1, bank[7])
                    pe.wait_ge(std_ready, norms_before(N_PHASES) + 1)
                for d in range(4, D_TILES):
                    m = pe.transpose(bank[4 + a][:, (d - 4) * P:(d - 3) * P], y[:, d, a * P:(a + 1) * P], ident[:])
                m.then_inc(y_turned, 1)

        @block.scalar
        def _(act):
            def split(slot, use, value=None):
                act.wait_ge(loaded[slot], loaded_value(slot, use) if value is None else value)
                if not isinstance(use, int) or use > 0:
                    act.wait_ge(unit_used[slot], use)
                act.activation(w_hi[slot], staged[slot][:], ACT.Copy).then_inc(split_hi[slot], 1)

            def root(q, src, out, n_features):
                act.wait_ge(sumsq_ready, q + 1)
                act.activation(out[:], src[:, 0:TOK_TILES], ACT.Sqrt, bias=eps[:], scale=1.0 / n_features)\
                   .then_inc(std_ready, 1)

            def copy_rstd(q, src, out):
                act.wait_ge(rstd_spread, q + 1)
                act.activation(out[:], src, ACT.Copy).then_inc(rstd_copied, 1)

            def norm_root(m):
                root(norms_before(m), bank[4], std, D_MODEL)

            def norm_copy(m):
                copy_rstd(norms_before(m), bank[5], rstd_b)

            def norm(m):
                last = m == N_PHASES
                for d in range(D_TILES):
                    gain = cols[:, ROW_NORM[m] + d:ROW_NORM[m] + d + 1]
                    act.wait_ge(h_added, OUT0[m] + d + 1)
                    if d == 0:
                        act.wait_ge(cols_ready, 1)
                    act.activation(y[:, d, :] if last else u_hi[:, d, :], h[:, d, :], ACT.Copy, scale=gain)\
                       .then_inc(y_ready if last else u_hi_ready, 1)
                    if d >= 3:
                        act.wait_ge(sq_summed, sums_before(m) + d - 2)
                    act.activation(sq_sum[:] if d == 0 else sq[:, d % 2, :], h[:, d, :], ACT.Square)\
                       .then_inc(squared, 1)

            def ffn_pair(ph, j, more=True, first=False):
                s, no = USES0[ph], FF_PAIRS * FFN_NO[ph]
                later = ph == N_PHASES - 1
                if first:
                    norm_root(ph)
                    split(0, s[0] + j + 1)
                    norm_copy(ph)
                for i in range(2):
                    act.wait_ge(a_scaled, 2 * no + 1 + i + j * 2)
                    if ph > 0 or not first:
                        act.wait_ge(silu_r_ready, 2 * no - 1 + i + j * 2)
                    act.activation(silu_a[:, i, :], a_scaled_t[:, i, :], ACT.Silu).then_inc(silu_ready, 1)
                if more and not first:
                    split(0, s[0] + j + 1)
                split(2, s[2] + j)
                for i in range(2):
                    act.wait_ge(hid_ready, 2 * no + 1 + i + j * 2)
                    act.activation(mid_hi[:, i, :], hid[:, i, :], ACT.Copy).then_inc(mid_hi_ready, 1)
                if more:
                    more_pieces = 16 * (KEY_PIECES - 1) * (NSA_GROUPS + 1)
                    split(1, s[1] + j + 1, value=(s[1] + 2) * 16 + j * 16 + more_pieces if later else None)

            def ffn(ph):
                ffn_pair(ph, 0, first=True)
                last = ph == N_PHASES - 1
                with act.Fori(1, FF_PAIRS - (1 if last else 0)) as j:
                    ffn_pair(ph, j)
                if last:
                    ffn_pair(ph, FF_PAIRS - 1, more=False)

            def retention_head(hd, first=False, last=False):
                s = USES0[RET_PHASE]

                def rotated_hi(n):
                    for i in range(2):
                        act.wait_ge(rotated, hd * 4 + (2 * n + i + 1))
                        act.activation(r_hi[n][:, i, :], r_g[:, 2 * i, :], ACT.Copy).then_inc(rot_hi, 1)

                split(2, s[2] + hd * 2)
                if first:
                    norm_root(RET_PHASE)
                split(0, s[0] + hd * 3 + 1)
                if first:
                    norm_copy(RET_PHASE)
                rotated_hi(0)
                split(1, s[1] + hd * 3 + 1)
                rotated_hi(1)
                split(2, s[2] + hd * 2 + 1)
                for a in range(TOK_TILES):
                    if a < TOK_TILES - 1:
                        act.wait_ge(v_ready, hd * 3 + a + 1)
                    else:
                        act.wait_ge(unit_used[0], s[0] + hd * 3 + 2)
                    if first and a == 0:
                        act.wait_ge(rstd_ready, RET_PHASE + 1)
                    act.activation(r_v[:, a, :], bank[4 + a], ACT.Copy, scale=rstd[:, a:a + 1]).then_inc(v_copied, 1)
                split(0, s[0] + hd * 3 + 2)
                for e in range(RET_E_TILES):
                    act.wait_ge(g_scaled, hd * 4 + e + 1)
                    act.activation(r_g[:, e, :], r_g[:, e, :], ACT.Silu).then_inc(silu_g_ready, 1)
                    if e == 1:
                        split(1, s[1] + hd * 3 + 2)
                for e in range(RET_E_TILES + 1):
                    if e < RET_E_TILES:
                        act.wait_ge(o_ready, hd * 4 + e + 1)
                        if e == 3:
                            act.wait_ge(sq_summed, 2 * (D_TILES - 1) + 1 + hd * 3)
                        act.activation(sq_sum[:] if e == 0 else sq[:, e % 2, :], bank[e], ACT.Square)\
                           .then_inc(squared, 1)
                    if e >= 1:
                        act.wait_ge(gated, hd * 4 + e)
                        act.activation(mid_hi[:, e - 1, :], r_g[:, e - 1, :], ACT.Copy).then_inc(z_hi_ready, 1)
                root(hd + 2, bank[3], std_g, RET_DV)
                copy_rstd(hd + 2, bank[3], rstd_gb)
                split(0, s[0] + hd * 3 + 3)
                if last:
                    norm(RET_PHASE + 1)
                split(1, s[1] + hd * 3 + 3)

            def compression():
                s = USES0[NSA_PHASE]

                def windows_hi(c, half):
                    rows = slice(half * D_TILES, (half + 1) * D_TILES)
                    act.wait_ge(cx_added, CMP_K_TILES * c + D_TILES * (half + 1))
                    if c == 1:
                        act.wait_ge(unit_used[1], s[1] + 2 + half)
                    act.activation(c_xhi[:, rows, :], c_x[:, rows, :], ACT.Copy).then_inc(cx_hi, 1)

                def silu_hidden(c):
                    act.wait_ge(unit_used[1 - c], s[1 - c] + 3)
                    if c == 1:
                        act.wait_ge(chid_turned, 1)
                    act.activation(c_hid_tok[0:N_WIN, :], bank[4 + c][0:N_WIN, 0:CMP_HID], ACT.Silu).then_inc(chid_silu, 1)

                split(2, s[2])
                norm_root(NSA_PHASE)
                split(0, s[0] + 1)
                act.wait_ge(unit_used[2], s[2] + 1)
                act.activation(gates_fm[0:N_GATES, :], bank[7][0:N_GATES, :], ACT.Copy).then_inc(gates_copied, 1)
                split(2, s[2] + 1)
                norm_copy(NSA_PHASE)
                act.wait_ge(gates_turned, 1)
                act.wait_ge(rstd_ready, norms_before(NSA_PHASE) + 1)
                for a in range(TOK_TILES):
                    act.activation(gates[:, a, :], bank[7][:, a * N_GATES:(a + 1) * N_GATES], ACT.Sigmoid,
                                   scale=rstd[:, a:a + 1]).then_inc(gates_set, 1)
                windows_hi(0, 0)
                windows_hi(0, 1)
                split(1, s[1] + 1)

                def copy_values(a):
                    if a < TOK_TILES - 1:
                        act.wait_ge(v_all_ready, a + 1)
                    else:
                        act.wait_ge(unit_used[0], s[0] + 2)
                    act.activation(v_all[:, a, :, :], bank[a].rearrange("p (b c) -> p b c", b=2), ACT.Copy,
                                   scale=rstd[:, a:a + 1]).then_inc(v_all_set, 1)

                copy_values(0)
                copy_values(1)
                split(1, s[1] + 2)
                windows_hi(1, 0)
                copy_values(2)
                windows_hi(1, 1)
                silu_hidden(0)
                split(2, s[2] + 2)
                split(0, s[0] + 2)
                copy_values(3)
                act.wait_ge(const_set, 5)
                act.wait_ge(ckv_ready, 1)
                act.activation(c_khi[:, :, 0:N_CMP], bank[7][:, 0:N_WIN].rearrange("p (g n) -> p g n", g=NSA_GROUPS),
                               ACT.Copy).then_inc(ck_hi, 1)
                split(1, s[1] + 3, value=loaded_value(1, None, group=0))
                silu_hidden(1)
                split(0, s[0] + 3)

            def nsa_group(g):
                s = USES0[NSA_PHASE]
                split(2, s[2] + g + NSA_FIRST[2])
                act.wait_ge(gk_scaled, g + 1)
                act.wait_ge(halves_zeroed, 5)
                for br in range(2):
                    for par in range(2):
                        act.activation(n_khi[par * NSA_DH:(par + 1) * NSA_DH, br, par, :],
                                       n_kf32[br * NSA_DH:(br + 1) * NSA_DH, :], ACT.Copy).then_inc(gk_hi, 1)
                split(1, s[1] + g + (NSA_FIRST[1] + 1), value=loaded_value(1, None, group=g + 1))
                for i in range(2):
                    act.wait_ge(gq_scaled, g * 2 + (i + 1))
                    act.activation(n_qhi[:, i, :], n_f32[:, i, :], ACT.Copy).then_inc(gq_hi, 1)
                def turned(n):
                    pair, ib, par = ITEMS[n]
                    act.wait_ge(pt_ready, g * (2 * N_ITEMS) + (2 * n + 1))
                    if n >= 2:
                        act.wait_ge(pv_done, g * N_ITEMS + (n - 1))
                    act.activation(n_pt[:, n % 2, 0, 0:width(ib)], bank[4][:, 0:width(ib)], ACT.Copy)\
                       .then_inc(pt_copied[0], 1)
                    if False:
                        act.wait_ge(pt_ready, g * (2 * N_ITEMS) + 2 * (n + 1))
                        if n >= 1:
                            act.wait_ge(pt_copied[1], g * N_ITEMS + n)
                        act.activation(n_pt[:, n % 2, 1, 0:width(ib)], bank[5][:, 0:width(ib)], ACT.Copy)\
                           .then_inc(pt_copied[1], 1)

                def exponents(n):
                    pair, ib, par = ITEMS[n]
                    act.wait_ge(s_biased, g * len(BATCHES) + (BATCH_OF[n] + 1))
                    if n >= 3:
                        act.wait_ge(pt_ready, g * (2 * N_ITEMS) + 2 * (n - 2))
                    for br in range(2):
                        c = slice(n % 4 * 2 + br, n % 4 * 2 + br + 1)
                        act.activation(n_p[:, n % 3, br, 0:width(ib)], item_scores(n)[:, br, :], ACT.Exp,
                                       bias=s_bias[:, c], scale=NSA_SCALE, accum_out=s_den[:, c]).then_inc(s_exp, 1)

                def o_hi(i):
                    act.wait_ge(pv_done, g * N_ITEMS + (i + 1) * (N_ITEMS // 2))
                    act.activation(mid_hi[:, i, :], bank[6 + i], ACT.Copy).then_inc(no_hi_ready, 1)

                exponents(0)
                exponents(1)
                for n in range(N_ITEMS):
                    turned(n)
                    if n + 2 < N_ITEMS:
                        exponents(n + 2)
                    if n == 0:
                        act.wait_ge(cs_steps, g * CS_STEPS + 6)
                        act.activation(c_p[:].rearrange("p a n -> p (a n)"), c_s[:].rearrange("p a n -> p (a n)"),
                                       ACT.Exp, scale=NSA_SCALE).then_inc(cs_exp, 1)
                    if n == LATE_ITEMS - 1:
                        act.wait_ge(cpt_ready, g + 1)
                        act.activation(c_pt.rearrange("p a q -> p (a q)"), bank[7], ACT.Copy).then_inc(cpt_copied, 1)
                    if n == N_ITEMS // 2 - 2:
                        split(0, s[0] + g + (NSA_FIRST[0] + 1))
                    if n == N_ITEMS // 2 + 2:
                        o_hi(0)
                o_hi(1)

            split(0, 0)
            norm(0)
            split(1, 0)
            ffn(0)
            norm(1)
            retention_head(0, first=True)
            with act.Fori(1, RET_HEADS - 1) as hd:
                retention_head(hd)
            retention_head(RET_HEADS - 1, last=True)
            ffn(2)
            norm(3)
            ffn(3)
            norm(4)
            compression()
            with act.Fori(0, NSA_GROUPS) as g:
                nsa_group(g)
            norm(5)
            ffn(5)
            norm(6)
            root(norms_before(N_PHASES), bank[7], std, D_MODEL)
            act.wait_ge(rstd_ready, norms_before(N_PHASES) + 1)
            for half in range(2):
                for a in range(0, TOK_TILES, 2):
                    act.wait_ge(y_turned, half * TOK_TILES + a + 1)
                    act.activation(x_tok[:, a, half * SEQ:(half + 1) * SEQ], bank[4 * half + a], ACT.Copy,
                                   scale=rstd[:, a:a + 1]).then_inc(y_copied[0], 1)

        @block.vector
        def _(dve):
            def split(slot, use, words=UNIT):
                dve.wait_ge(split_hi[slot], use + 1)
                dve.tensor_tensor(w_lo[slot], staged[slot][:], w_hi[slot].bitcast(F32), ALU.subtract)\
                   .then_inc(split_lo[slot], 1)

            def invert(q, src, out):
                dve.wait_ge(std_ready, q + 1)
                dve.reciprocal(out[:], src[:]).then_inc(rstd_ready, 1)

            def low(m, d):
                dve.wait_ge(u_hi_ready, D_TILES * m + d + 1)
                dve.scalar_tensor_tensor(out=u_lo[:, d, :], in0=h[:, d, :],
                                         scalar=cols[:, ROW_NORM[m] + d:ROW_NORM[m] + d + 1],
                                         in1=u_hi[:, d, :].bitcast(F32), op0=ALU.mult, op1=ALU.subtract)\
                   .then_inc(u_ready, 1)

            def add_out(ph, group, bank_of, slot, use, scale, final=False):
                for d in range(D_TILES):
                    if d < D_TILES - 1:
                        dve.wait_ge(out_ready, OUT_READY0[ph] + d + 1 + group * (D_TILES - 1))
                    else:
                        dve.wait_ge(unit_used[slot], use + 1)
                    dve.wait_ge(h_added, OUT0[ph] + d + 1 + group * D_TILES)
                    dve.scalar_tensor_tensor(out=h[:, d, :], in0=bank[bank_of(d)], scalar=scale, in1=h[:, d, :],
                                             op0=ALU.mult, op1=ALU.add).then_inc(h_added, 1)
                    if final and d >= 1:
                        low(ph + 1, d - 1)
                if final:
                    low(ph + 1, D_TILES - 1)

            def ffn_pair(ph, j, more=True, first=False):
                s, no = USES0[ph], FF_PAIRS * FFN_NO[ph]
                if first:
                    invert(norms_before(ph), std, rstd)
                    split(0, s[0] + j + 1)
                    dve.wait_ge(rstd_copied, norms_before(ph) + 1)
                for i in range(2):
                    if i == 0:
                        dve.wait_ge(a_ready, no + j + 1)
                    else:
                        dve.wait_ge(unit_used[0], s[0] + j + 1)
                    if ph > 0 or not first:
                        dve.wait_ge(silu_ready, 2 * no - 1 + i + j * 2)
                    dve.tensor_tensor(a_scaled_t[:, i, :], bank[i], rstd_b[:], ALU.mult).then_inc(a_scaled, 1)
                if not first:
                    ffn_out(ph, j - 1)
                    if more:
                        split(0, s[0] + j + 1)
                split(2, s[2] + j)
                if ph > 0 or not first:
                    dve.wait_ge(mid_ready, 2 * no + j * 2)
                for i in range(2):
                    dve.wait_ge(silu_r_ready, 2 * no + 1 + i + j * 2)
                    if i == 0:
                        dve.wait_ge(b_ready, no + j + 1)
                    else:
                        dve.wait_ge(unit_used[1], s[1] + j + 1)
                    dve.tensor_tensor(hid[:, i, :], silu_r[:, i, :], bank[2 + i], ALU.mult).then_inc(hid_ready, 1)
                    dve.wait_ge(mid_hi_ready, 2 * no + 1 + i + j * 2)
                    dve.tensor_tensor(mid_lo[:, i, :], hid[:, i, :], mid_hi[:, i, :].bitcast(F32), ALU.subtract)\
                       .then_inc(mid_ready, 1)
                if more:
                    split(1, s[1] + j + 1)

            def ffn_out(ph, i, final=False):
                add_out(ph, i, lambda d: 4 + d % 4, 2, USES0[ph][2] + i, 0.5, final)

            def ffn(ph):
                ffn_pair(ph, 0, first=True)
                last = ph == N_PHASES - 1
                with dve.Fori(1, FF_PAIRS - (1 if last else 0)) as j:
                    ffn_pair(ph, j)
                if last:
                    ffn_pair(ph, FF_PAIRS - 1, more=False)
                ffn_out(ph, FF_PAIRS - 1, final=not last)

            def retention_head(hd, first=False, last=False):
                s = USES0[RET_PHASE]

                def rotate(n, x):
                    prods = ((0, x[0], cos_t), (1, x[1], sin_t), (2, x[0], sin_t), (3, x[1], cos_t))
                    dve.wait_ge(qk_ready, hd * 2 + n + 1)
                    dve.wait_ge(unit_used[n], s[n] + hd * 3 + 1)
                    dve.wait_ge(tables_scaled, 2)
                    if n == 0:
                        if not first:
                            dve.wait_ge(z_ready, hd * 4)
                    else:
                        dve.wait_ge(rot_ready, hd * 4 + 2)
                    for i, b, table in prods:
                        dve.tensor_tensor(r_g[:, i, :], b, table, ALU.mult).then_inc(rot_products, 1)
                    dve.wait_ge(rot_products, hd * 8 + (4 * n + 4))
                    dve.tensor_tensor(r_g[:, 0, :], r_g[:, 0, :], r_g[:, 1, :], ALU.subtract).then_inc(rotated, 1)
                    dve.tensor_tensor(r_g[:, 2, :], r_g[:, 2, :], r_g[:, 3, :], ALU.add).then_inc(rotated, 1)
                    for i in range(2):
                        dve.wait_ge(rot_hi, hd * 4 + (2 * n + i + 1))
                        dve.tensor_tensor(r_lo[n][:, i, :], r_g[:, 2 * i, :], r_hi[n][:, i, :].bitcast(F32), ALU.subtract)\
                           .then_inc(rot_ready, 1)

                split(2, s[2] + hd * 2)
                if first:
                    invert(norms_before(RET_PHASE), std, rstd)
                split(0, s[0] + hd * 3 + 1)
                rotate(0, bank[0:2])
                split(1, s[1] + hd * 3 + 1)
                rotate(1, bank[2:4])
                split(2, s[2] + hd * 2 + 1)
                for jb in range(TOK_TILES):
                    n = SEQ - jb * P
                    dve.wait_ge(scores_ready, hd * 4 + jb + 1)
                    dve.tensor_tensor(r_p[:, r_p_at[jb]:r_p_at[jb] + n], bank[jb][:, 0:n],
                                      decay[:, part(hd * SEQ, n)],
                                      ALU.mult).then_inc(decayed, 1)
                split(0, s[0] + hd * 3 + 2)
                for e in range(RET_E_TILES):
                    if e % 2 == 0:
                        dve.wait_ge(g_ready, hd * 2 + (e // 2 + 1))
                    elif e == 1:
                        dve.wait_ge(unit_used[1], s[1] + hd * 3 + 2)
                    else:
                        dve.wait_ge(unit_used[2], s[2] + hd * 2 + 2)
                    dve.tensor_tensor(r_g[:, e, :], bank[4 + e], rstd_b[:], ALU.mult).then_inc(g_scaled, 1)
                    if e == 1:
                        split(1, s[1] + hd * 3 + 2)
                for e in range(RET_E_TILES + 1):
                    if e < RET_E_TILES:
                        gain = ROW_GN + e
                        dve.wait_ge(silu_g_ready, hd * 4 + e + 1)
                        dve.wait_ge(squared, 2 * D_TILES + e + 1 + hd * RET_E_TILES)
                        dve.scalar_tensor_tensor(out=r_g[:, e, :], in0=bank[e],
                                                 scalar=cols[:, part(hd * 4 + gain, 1)],
                                                 in1=r_g[:, e, :], op0=ALU.mult, op1=ALU.mult).then_inc(gated, 1)
                    if e >= 1:
                        dve.wait_ge(z_hi_ready, hd * 4 + e)
                        dve.tensor_tensor(mid_lo[:, e - 1, :], r_g[:, e - 1, :], mid_hi[:, e - 1, :].bitcast(F32),
                                          ALU.subtract).then_inc(z_ready, 1)
                invert(hd + 2, std_g, rstd_g)

                def scaled(d):
                    if d < D_TILES - 1:
                        dve.wait_ge(out_ready, OUT_READY0[RET_PHASE] + d + 1 + hd * (D_TILES - 1))
                    else:
                        dve.wait_ge(unit_used[1], s[1] + hd * 3 + 3)
                    if not first or d >= 2:
                        dve.wait_ge(h_added, OUT0[RET_PHASE] + D_TILES + (d - 1) + hd * D_TILES)
                    dve.tensor_tensor(r_out[:, d % 2, :], bank[RET_OUT_BANK[d]], rstd_gb[:], ALU.mult)\
                       .then_inc(out_scaled, 1)

                dve.wait_ge(rstd_copied, hd + 3)
                scaled(0)
                for d in range(D_TILES):
                    if d + 1 < D_TILES:
                        scaled(d + 1)
                    if d == 2:
                        split(0, s[0] + hd * 3 + 3)
                    dve.wait_ge(out_scaled, d + 1 + hd * D_TILES)
                    dve.wait_ge(h_added, OUT0[RET_PHASE] + d + 1 + hd * D_TILES)
                    dve.tensor_tensor(h[:, d, :], h[:, d, :], r_out[:, d % 2, :], ALU.add).then_inc(h_added, 1)
                    if last and d >= 1:
                        low(RET_PHASE + 1, d - 1)
                if last:
                    low(RET_PHASE + 1, D_TILES - 1)
                split(1, s[1] + hd * 3 + 3)

            def compression():
                s = USES0[NSA_PHASE]

                def windows(c):
                    if c == 1:
                        dve.wait_ge(cx_added, CMP_K_TILES)
                    for g in range(NSA_GROUPS):
                        if g == 0:
                            dve.wait_ge(ct_ready, c + 1)
                        elif g == 2:
                            dve.wait_ge(unit_used[c], s[c] + 1)
                        b = bank[2 * c + g // 2][g % 2 * NSA_DH:(g % 2 + 1) * NSA_DH, :]
                        r = rstd_b[g % 2 * NSA_DH:(g % 2 + 1) * NSA_DH, :]
                        dve.tensor_tensor(c_t[0:NSA_DH, g, :], b, r, ALU.mult).then_inc(ct_copied, 1)
                        dve.tensor_tensor(c_t[NSA_DH:P, g, 0:SEQ - 1], b[:, 1:SEQ], r[:, 1:SEQ], ALU.mult)\
                           .then_inc(ct_copied, 1)
                    dve.wait_ge(ct_copied, 8 * (c + 1))
                    if c == 1:
                        dve.wait_ge(cx_split, 2)
                    for kk in range(CMP_K_TILES):
                        col = ROW_POS + c * CMP_K_TILES + kk
                        dve.tensor_scalar(c_x[:, kk, :].rearrange("p (g n) -> p g n", g=NSA_GROUPS),
                                          c_t[:, :, 2 * kk:2 * kk + CMP_STRIDE * (N_CMP - 1) + 1:CMP_STRIDE],
                                          cols[:, col:col + 1], None, ALU.add).then_inc(cx_added, 1)

                def windows_lo(c, half):
                    rows = slice(half * D_TILES, (half + 1) * D_TILES)
                    dve.wait_ge(cx_hi, 2 * c + half + 1)
                    dve.wait_ge(cx_added, CMP_K_TILES * c + D_TILES * (half + 1))
                    dve.tensor_tensor(c_xlo[:, rows, :], c_x[:, rows, :], c_xhi[:, rows, :].bitcast(F32), ALU.subtract)\
                       .then_inc(cx_split, 1)

                def hidden_copied(c):
                    dve.wait_ge(chid_turned, c + 1)
                    if c == 1:
                        dve.wait_ge(ckv_ready, 1)
                    dve.tensor_copy(c_hid[:], bank[6][:, 0:2 * N_WIN].rearrange("p (a n) -> p a n", a=2))\
                       .then_inc(chid_copied, 1)

                split(2, s[2])
                invert(norms_before(NSA_PHASE), std, rstd)
                split(0, s[0] + 1)
                split(2, s[2] + 1)
                dve.wait_ge(rstd_copied, norms_before(NSA_PHASE) + 1)
                windows(0)
                windows_lo(0, 0)
                windows_lo(0, 1)
                split(1, s[1] + 1)
                windows(1)
                split(1, s[1] + 2)
                windows_lo(1, 0)
                windows_lo(1, 1)
                hidden_copied(0)
                split(2, s[2] + 2)
                split(0, s[0] + 2)
                dve.wait_ge(const_set, 5)
                dve.wait_ge(ck_hi, 1)
                dve.tensor_tensor(c_klo[:, :, 0:N_CMP], bank[7][:, 0:N_WIN].rearrange("p (g n) -> p g n", g=NSA_GROUPS),
                                  c_khi[:, :, 0:N_CMP].bitcast(F32), ALU.subtract).then_inc(ckv_copied, 1)
                split(1, s[1] + 3)
                hidden_copied(1)
                dve.wait_ge(ckv_ready, 2)
                dve.tensor_copy(c_v[0:N_CMP, :, :],
                                bank[7][0:N_CMP, 0:NSA_GROUPS * NSA_DH].rearrange("p (g d) -> p g d", g=NSA_GROUPS))\
                   .then_inc(ckv_copied, 1)
                split(0, s[0] + 3)

            def nsa_group(g):
                s = USES0[NSA_PHASE]
                dve.wait_ge(halves_zeroed, 5)
                dve.wait_ge(const_derived, 3)
                dve.wait_ge(ckv_copied, 2)
                dve.wait_ge(gates_set, 4)
                for of, to in ((c_khi, c_kghi), (c_klo, c_kglo)):
                    for par in range(2):
                        r = slice(par * NSA_DH, (par + 1) * NSA_DH)
                        dve.tensor_copy(to[r, par, :], of[r, ds(g, 1), :].rearrange("p a n -> p (a n)"))\
                           .then_inc(group_set, 1)
                for ib in range(TOK_TILES):
                    dve.tensor_copy(c_vg[ib * CMP_PAD:(ib + 1) * CMP_PAD, ib, :],
                                    c_v[:, ds(g, 1), :].rearrange("p a n -> p (a n)")).then_inc(group_set, 1)
                dve.wait_ge(v_all_set, TOK_TILES)
                dve.tensor_copy(n_v.rearrange("p a b d -> p (a b) d"),
                                v_all[:, :, :, ds(g * NSA_DH, NSA_DH)].rearrange("p a b d -> p (a b) d"))\
                   .then_inc(group_set, 1)
                for br in range(3):
                    dve.tensor_copy(gate_g[:, br, :].rearrange("p (b a i) -> p b a i", b=2, a=2),
                                    gates[:, :, ds(g * NSA_HPG + br * NSA_HEADS, NSA_HPG)]
                                    .rearrange("p i (a b) -> p b a i", b=2)).then_inc(group_set, 1)
                dve.wait_ge(unit_used[1], s[1] + g + (NSA_FIRST[1] + 1))
                dve.tensor_tensor(n_kf32, bank[0], rstd_b[:], ALU.mult).then_inc(gk_scaled, 1)
                split(2, s[2] + g + NSA_FIRST[2])
                dve.wait_ge(gk_hi, g * 4 + 4)
                for n in range(2):
                    r = slice(n * NSA_DH, (n + 1) * NSA_DH)
                    dve.tensor_tensor(n_klo[r, n, n, :], n_kf32[r, :], n_khi[r, n, n, :].bitcast(F32), ALU.subtract)\
                       .then_inc(gk_split, 1)
                dve.wait_ge(gk_split, g * 4 + 2)
                for n in range(2):
                    r, other = slice(n * NSA_DH, (n + 1) * NSA_DH), slice((1 - n) * NSA_DH, (2 - n) * NSA_DH)
                    dve.tensor_copy(n_klo[other, n, 1 - n, :], n_klo[r, n, n, :]).then_inc(gk_split, 1)
                for i in range(2):
                    if i == 0:
                        dve.wait_ge(gq_ready, g + 1)
                    else:
                        dve.wait_ge(unit_used[0], s[0] + g + (NSA_FIRST[0] + 1))
                    dve.tensor_tensor(n_f32[:, i, :], bank[2 + i], rstd_b[:], ALU.mult).then_inc(gq_scaled, 1)
                    dve.wait_ge(gq_hi, g * 2 + (i + 1))
                    dve.tensor_tensor(n_qlo[:, i, :], n_f32[:, i, :], n_qhi[:, i, :].bitcast(F32), ALU.subtract)\
                       .then_inc(gq_split, 1)
                    if i == 0:
                        split(1, s[1] + g + (NSA_FIRST[1] + 1))

                steps = g * CS_STEPS

                def flat(v):
                    return v.rearrange("p a n -> p (a n)")

                def over_keys(v):
                    return v.unsqueeze(2).to_broadcast([P, 16, CMP_PAD])

                def largest(b):
                    pair, ib, pars = BATCHES[b]
                    n = BATCH_OF.index(b)
                    c = slice(n % 4 * 2, (n % 4 + len(pars)) * 2)
                    dve.wait_ge(s_ready, g * (2 * N_ITEMS) + 2 * (batch_end(n) + 1))
                    dve.reduce_max(s_max[:, c].rearrange("p (a b) -> p a b", b=2),
                                   banks2[b % 2][:, :, 0:len(pars) * width(ib)]
                                   .rearrange("p b (a n) -> p a b n", a=len(pars)), AX_X).then_inc(s_maxed, 1)
                    dve.wait_ge(s_maxed, g * len(BATCHES) + (b + 1))
                    dve.tensor_scalar(s_bias[:, c], s_max[:, c], -NSA_SCALE, None, ALU.mult).then_inc(s_biased, 1)

                def weigh(n):
                    pair, ib, par = ITEMS[n]
                    c = n % 4 * 2
                    at = (par * 2 + pair) * TOK_TILES + ib
                    dve.wait_ge(s_exp, g * (2 * N_ITEMS) + 2 * (n + 1))
                    dve.reciprocal(s_rden[:, c:c + 2], s_den[:, c:c + 2]).then_inc(s_recip, 1)
                    dve.wait_ge(s_recip, g * N_ITEMS + (n + 1))
                    for br in range(2):
                        dve.tensor_scalar(n_p[:, n % 3, br, 0:width(ib)], n_p[:, n % 3, br, 0:width(ib)],
                                          s_rden[:, c + br:c + br + 1], gate_g[:, br + 1, at:at + 1], ALU.mult, ALU.mult)\
                           .then_inc(p_ready, 1)

                def turned(n):
                    pair, ib, par = ITEMS[n]
                    if False:
                        return
                    dve.wait_ge(pt_ready, g * (2 * N_ITEMS) + 2 * (n + 1))
                    if n >= 1:
                        dve.wait_ge(pt_copied[1], g * N_ITEMS + n)
                    if n >= 2:
                        dve.wait_ge(pv_done, g * N_ITEMS + (n - 1))
                    dve.tensor_copy(n_pt[:, n % 2, 1, 0:width(ib)], bank[5][:, 0:width(ib)]).then_inc(pt_copied[1], 1)

                def o_lo(i):
                    dve.wait_ge(no_hi_ready, g * 2 + (i + 1))
                    dve.tensor_tensor(mid_lo[:, i, :], bank[6 + i], mid_hi[:, i, :].bitcast(F32), ALU.subtract)\
                       .then_inc(no_split, 1)

                def compressed_added():
                    dve.wait_ge(cs_ready, g + 1)
                    for par in range(2):
                        for pair in range(2):
                            at = 8 * par + 4 * pair
                            dve.tensor_tensor(c_s[:, at:at + 4, :], bank[4][:, 2 * P * pair:2 * P * (pair + 1)]
                                              .rearrange("p (i a n) -> p i a n", i=TOK_TILES, a=2)[:, :, par, :],
                                              cmp_neg[:], ALU.add).then_inc(cs_steps, 1)

                def compressed_lowered():
                    dve.wait_ge(cs_steps, steps + 4)
                    dve.reduce_max(c_max, c_s, AX_X).then_inc(cs_steps, 1)
                    dve.wait_ge(cs_steps, steps + 5)
                    dve.tensor_tensor(c_s, c_s, over_keys(c_max), ALU.subtract).then_inc(cs_steps, 1)

                def compressed_summed():
                    by_head = "p (r i) n -> p r (i n)"
                    dve.wait_ge(cs_exp, g + 1)
                    dve.tensor_tensor(c_p[:].rearrange(by_head, r=4), c_p[:].rearrange(by_head, r=4),
                                      flat(cmp_mask[:]).unsqueeze(1).to_broadcast([P, 4, P]), ALU.mult).then_inc(cs_steps, 1)
                    dve.wait_ge(cs_steps, steps + 7)
                    dve.reduce_sum(c_den, c_p, AX_X).then_inc(cs_steps, 1)

                def compressed_weighed():
                    dve.wait_ge(cs_steps, steps + 8)
                    dve.tensor_scalar(c_den, c_den, 1e-30, None, ALU.max).then_inc(cs_steps, 1)
                    dve.wait_ge(cs_steps, steps + 9)
                    dve.reciprocal(c_rden, c_den).then_inc(cs_steps, 1)
                    dve.wait_ge(cs_steps, steps + 10)
                    dve.wait_ge(group_set, g * GROUP_SETS + GROUP_SETS)
                    dve.tensor_tensor(c_fac, c_rden, gate_g[:, 0, :], ALU.mult).then_inc(cs_steps, 1)
                    dve.wait_ge(cs_steps, steps + 11)
                    dve.tensor_tensor(c_p, c_p, over_keys(c_fac), ALU.mult).then_inc(cs_steps, 1)

                largest(0)
                compressed_added()
                weigh(0)
                for n in range(N_ITEMS):
                    if n + 2 < N_ITEMS and BATCH_OF[n + 2] > BATCH_OF[n + 1]:
                        largest(BATCH_OF[n + 2])
                    if n + 1 < N_ITEMS:
                        weigh(n + 1)
                    if n == N_ITEMS // 2 - 1:
                        split(0, s[0] + g + (NSA_FIRST[0] + 1))
                    if n == 0:
                        compressed_lowered()
                    turned(n)
                    if n == 1:
                        compressed_summed()
                    if n == 2:
                        compressed_weighed()
                    if n == N_ITEMS // 2 + 3:
                        o_lo(0)
                o_lo(1)
                add_out(NSA_PHASE, g, lambda d: d % 4, 2, s[2] + g + NSA_FIRST[2], 1.0)

            dve.wait_ge(rows_turned, 1)
            dve.tensor_copy(cols[:], bank[7][:, 0:N_ROWS]).then_inc(cols_ready, 1)
            dve.wait_ge(cols_ready, 1)
            split(0, 0)
            for d in range(D_TILES):
                dve.wait_ge(x_turned, d + 1)
                dve.tensor_copy(h[:, d, :], bank[d]).then_inc(h_added, 1)
                if d > 0:
                    low(0, d - 1)
            low(0, D_TILES - 1)
            split(1, 0)
            dve.wait_ge(const_loaded, 16 * 6)
            dve.tensor_copy(ident_bf[:], ident[:]).then_inc(const_derived, 1)
            dve.tensor_copy(causal_neg_bf[:], causal_neg[:]).then_inc(const_derived, 1)
            dve.tensor_scalar(cmp_neg[:], cmp_mask[:], -1.0, -NEG_RAW, ALU.add, ALU.mult).then_inc(const_derived, 1)
            ffn(0)
            retention_head(0, first=True)
            with dve.Fori(1, RET_HEADS - 1) as hd:
                retention_head(hd)
            retention_head(RET_HEADS - 1, last=True)
            ffn(2)
            ffn(3)
            compression()
            with dve.Fori(0, NSA_GROUPS) as g:
                nsa_group(g)
            for d in range(D_TILES):
                low(5, d)
            ffn(5)
            invert(norms_before(N_PHASES), std, rstd)
            dve.wait_ge(rstd_ready, norms_before(N_PHASES) + 1)
            for half in range(2):
                for a in range(1, TOK_TILES, 2):
                    dve.wait_ge(y_turned, half * TOK_TILES + a + 1)
                    dve.tensor_scalar(x_tok[:, a, half * SEQ:(half + 1) * SEQ], bank[4 * half + a], rstd[:, a:a + 1],
                                      None, ALU.mult).then_inc(y_copied[1], 1)

        @block.gpsimd
        def _(pool):
            def sum_tiles(squares, sums, n_tiles):
                for d in range(1, n_tiles):
                    pool.wait_ge(squared, squares + (d + 1))
                    if d > 1:
                        pool.wait_ge(sq_summed, sums + (d - 1))
                    pool.tensor_tensor(sq_sum[:], sq_sum[:], sq[:, d % 2, :], ALU.add).then_inc(sq_summed, 1)

            def norm(m):
                sum_tiles(squares_before(m), sums_before(m), D_TILES)

            def ffn_pair(ph, j):
                no = FF_PAIRS * FFN_NO[ph]
                for i in range(2):
                    pool.wait_ge(silu_ready, 2 * no + 1 + i + j * 2)
                    if ph > 0 or not isinstance(j, int):
                        pool.wait_ge(hid_ready, 2 * no - 1 + i + j * 2)
                    pool.tensor_tensor(silu_r[:, i, :], silu_a[:, i, :], rstd_b[:], ALU.mult).then_inc(silu_r_ready, 1)

            def ffn(ph):
                norm(ph)
                pool.wait_ge(rstd_copied, norms_before(ph) + 1)
                ffn_pair(ph, 0)
                with pool.Fori(1, FF_PAIRS) as j:
                    ffn_pair(ph, j)

            pool.memset(ones[:], 1.0).then_inc(const_set, 1)
            pool.memset(eps[:], NORM_EPS).then_inc(const_set, 1)
            pool.memset(c_khi[:].bitcast(F32), 0.0).then_inc(const_set, 1)
            pool.memset(c_klo[:].bitcast(F32), 0.0).then_inc(const_set, 1)
            pool.memset(c_v[:], 0.0).then_inc(const_set, 1)
            ffn(0)
            norm(RET_PHASE)
            pool.wait_ge(ret_loaded, 48)
            pool.wait_ge(rstd_copied, norms_before(RET_PHASE) + 1)
            pool.tensor_tensor(cos_t, cos_t, rstd_b[:], ALU.mult).then_inc(tables_scaled, 1)
            pool.tensor_tensor(sin_t, sin_t, rstd_b[:], ALU.mult).then_inc(tables_scaled, 1)
            with pool.Fori(0, RET_HEADS) as hd:
                sum_tiles(2 * D_TILES + hd * RET_E_TILES, 2 * (D_TILES - 1) + hd * (RET_E_TILES - 1), RET_E_TILES)
            ffn(2)
            ffn(3)
            norm(NSA_PHASE)
            pool.wait_ge(unit_used[0], USES0[NSA_PHASE][0] + 3)
            for zeroed in (n_khi, n_klo, c_kghi, c_kglo):
                pool.memset(zeroed.bitcast(F32), 0.0).then_inc(halves_zeroed, 1)
            pool.memset(c_vg, 0.0).then_inc(halves_zeroed, 1)
            ffn(5)
            norm(N_PHASES)


_INS = ["x", "norm_ffn1", "ffn1_w_in", "ffn1_w_out", "norm_mix", "norm_ffn2", "ffn2_w_in", "ffn2_w_out", "norm_final",
        "ret_w_in", "ret_gn_gain", "ret_w_out",
        "nsa_w_in", "nsa_cmp_pos", "nsa_cmp_w1", "nsa_cmp_w2", "nsa_w_out"]


def shape_constants():
    half = RET_DK // 2
    inv = np.float32(10000.0) ** (-np.arange(half, dtype=np.float32) / np.float32(half))
    ang = inv.astype(np.float32)[:, None] * np.arange(SEQ, dtype=np.float32)[None, :]
    log_gamma = np.log1p(-np.exp2(-5.0 - np.arange(RET_HEADS, dtype=np.float64)))
    rel = np.arange(SEQ)[None, :] - np.arange(P)[:, None]
    decay = np.where(rel >= 0, np.exp(np.maximum(rel, 0) * log_gamma[:, None, None]), 0.0) * RET_DK ** -0.5
    q = np.arange(SEQ).reshape(TOK_TILES, P).T
    n = np.arange(CMP_PAD)
    cmp_mask = (n * CMP_STRIDE + CMP_LEN - 1 <= q[:, :, None]) & (n < N_CMP)
    causal = np.where(np.arange(P)[None, :] <= np.arange(P)[:, None], 0.0, NEG_RAW)
    return {
        "c_ident": np.eye(P, dtype=np.float32),
        "c_cos": np.cos(ang).astype(np.float32),
        "c_sin": np.sin(ang).astype(np.float32),
        "c_decay": np.ascontiguousarray(decay.transpose(1, 0, 2).reshape(P, RET_HEADS * SEQ), dtype=np.float32),
        "c_causal": causal.astype(np.float32),
        "c_cmp_mask": cmp_mask.astype(np.float32),
    }


def kernel(**inputs):
    import concourse.bacc as bacc
    from concourse.bass_utils import run_bass_kernel_spmd

    nc = bacc.Bacc("TRN2", target_bir_lowering=False, num_devices=1)
    arrays = {name: np.ascontiguousarray(inputs[name]) for name in _INS}
    arrays.update(shape_constants())
    t = {name: nc.dram_tensor("in_" + name, a.shape, mybir.dt.from_np(a.dtype), kind="ExternalInput").ap()
         for name, a in arrays.items()}
    t["out"] = nc.dram_tensor("out_y", (1, SEQ, D_MODEL), F32, kind="ExternalOutput").ap()
    build(nc, t)
    r = run_bass_kernel_spmd(nc, [{"in_" + name: a for name, a in arrays.items()}], core_ids=[0])
    return r.results[0]["out_y"]
```
